# Optimizing a Trainium2 kernel written in Bass

```python
import math
import jax
import jax.numpy as jnp
from jax import lax
import numpy as np

D_MODEL = 1024
BATCH = 1
SEQ = 256
DEPTH = 2
DEC_BATCH = 8
DEC_SEQ = 1
PAST_LEN = 2048
PAGE_SIZE = 128

S5_WIDTH = D_MODEL // 2
S5_GROUP = 16
S5_GROUPS = S5_WIDTH // S5_GROUP
S5_STATE = 64
RET_HEADS = 4
RET_DK = 128
RET_DV = 256
RET_QK = RET_HEADS * RET_DK
RET_V = RET_HEADS * RET_DV
RET_CHUNK = 128
ROPE_BASE = 10000.0
CONV_WIDTH = D_MODEL // 2
CONV_K = 31
D_FF = 2816
N_EXPERTS = 8
TOP_K = 2
D_FF_EXPERT = 3584
N_DENSE = (DEPTH + 1) // 2
N_MOE = DEPTH // 2
N_BRANCH = 3
EPS = 1e-6
OFF_S5 = 0
OFF_Q = OFF_S5 + S5_WIDTH
OFF_K = OFF_Q + RET_QK
OFF_V = OFF_K + RET_QK
OFF_G = OFF_V + RET_V
OFF_CONV = OFF_G + RET_V
OFF_GATE = OFF_CONV + 2 * CONV_WIDTH
N_IN = OFF_GATE + N_BRANCH * D_MODEL

kernel_name = "hybrid_s5_retention_conformer_moe_step"

def rmsnorm(x, g):
    xf = x.astype(jnp.float32)
    y = xf * lax.rsqrt(jnp.mean(xf * xf, axis=-1, keepdims=True) + EPS)
    return (y * g.astype(jnp.float32)).astype(x.dtype)

def s5_discretize(lam_re, lam_im, log_dt, b_re, b_im):
    dt = jnp.exp(log_dt)[:, None]
    mag = jnp.exp(lam_re * dt)
    ang = lam_im * dt
    lbar_re = mag * jnp.cos(ang)
    lbar_im = mag * jnp.sin(ang)
    den = lam_re * lam_re + lam_im * lam_im
    nr = lbar_re - 1.0
    f_re = (nr * lam_re + lbar_im * lam_im) / den
    f_im = (lbar_im * lam_re - nr * lam_im) / den
    bbar_re = f_re[..., None] * b_re - f_im[..., None] * b_im
    bbar_im = f_re[..., None] * b_im + f_im[..., None] * b_re
    return lbar_re, lbar_im, bbar_re, bbar_im

def _complex_affine_combine(e1, e2):
    a1r, a1i, b1r, b1i = e1
    a2r, a2i, b2r, b2i = e2
    return (a2r * a1r - a2i * a1i,
            a2r * a1i + a2i * a1r,
            a2r * b1r - a2i * b1i + b2r,
            a2r * b1i + a2i * b1r + b2i)

def s5_branch(u, h0_re, h0_im, lam_re, lam_im, log_dt, b_re, b_im, c_re, c_im, d_skip, glu_w, glu_b):
    f32 = jnp.float32
    bsz, seq_len, _ = u.shape
    uf = u.astype(f32)
    lbar_re, lbar_im, bbar_re, bbar_im = s5_discretize(
        lam_re.astype(f32), lam_im.astype(f32), log_dt.astype(f32), b_re.astype(f32), b_im.astype(f32))
    ug = uf.reshape(bsz, seq_len, S5_GROUPS, S5_GROUP)
    bu_re = jnp.einsum("blgp,gnp->blgn", ug, bbar_re)
    bu_im = jnp.einsum("blgp,gnp->blgn", ug, bbar_im)
    a_re = jnp.broadcast_to(lbar_re, bu_re.shape)
    a_im = jnp.broadcast_to(lbar_im, bu_im.shape)
    acc_re, acc_im, hs_re, hs_im = lax.associative_scan(
        _complex_affine_combine, (a_re, a_im, bu_re, bu_im), axis=1)
    h0r = h0_re.astype(f32)[:, None]
    h0i = h0_im.astype(f32)[:, None]
    h_re = acc_re * h0r - acc_im * h0i + hs_re
    h_im = acc_re * h0i + acc_im * h0r + hs_im
    y = (jnp.einsum("blgn,gpn->blgp", h_re, c_re.astype(f32))
         - jnp.einsum("blgn,gpn->blgp", h_im, c_im.astype(f32))).reshape(bsz, seq_len, S5_WIDTH)
    y = y + d_skip.astype(f32) * uf
    z = jax.nn.gelu(y)
    out = z * jax.nn.sigmoid(z @ glu_w.astype(f32) + glu_b.astype(f32))
    return out, h_re[:, -1], h_im[:, -1]

def rotary(x, pos):
    half = RET_DK // 2
    freqs = ROPE_BASE ** (-jnp.arange(half, dtype=jnp.float32) / half)
    ang = pos[:, None] * freqs[None, :]
    cos = jnp.cos(ang)[None, :, None, :]
    sin = jnp.sin(ang)[None, :, None, :]
    x1 = x[..., :half]
    x2 = x[..., half:]
    return jnp.concatenate([x1 * cos - x2 * sin, x2 * cos + x1 * sin], axis=-1)

def retention_chunk(state, q, k, v, log_gamma):
    c = q.shape[2]
    idx = jnp.arange(c, dtype=jnp.float32)
    diff = idx[:, None] - idx[None, :]
    decay = jnp.where(diff >= 0, jnp.exp(jnp.maximum(diff, 0.0)[None] * log_gamma[:, None, None]), 0.0)
    inner = jnp.einsum("bhid,bhjd->bhij", q, k) * decay
    cross_decay = jnp.exp((idx + 1.0)[None, :] * log_gamma[:, None])[None, :, :, None]
    out = jnp.einsum("bhij,bhjv->bhiv", inner, v) + jnp.einsum("bhid,bhdv->bhiv", q, state) * cross_decay
    k_decay = jnp.exp((c - 1.0 - idx)[None, :] * log_gamma[:, None])[None, :, :, None]
    new_state = (jnp.exp(c * log_gamma)[None, :, None, None] * state
                 + jnp.einsum("bhjd,bhjv->bhdv", k * k_decay, v))
    return new_state, out

def retention_branch(q, k, v, g, state0, pos_offset):
    f32 = jnp.float32
    bsz, seq_len, _ = q.shape
    pos = jnp.arange(seq_len, dtype=f32) + pos_offset
    qh = rotary(q.astype(f32).reshape(bsz, seq_len, RET_HEADS, RET_DK), pos)
    kh = rotary(k.astype(f32).reshape(bsz, seq_len, RET_HEADS, RET_DK), pos) * (RET_DK ** -0.5)
    vh = v.astype(f32).reshape(bsz, seq_len, RET_HEADS, RET_DV)
    log_gamma = jnp.log(1.0 - 2.0 ** (-5.0 - jnp.arange(RET_HEADS, dtype=f32)))
    chunk = RET_CHUNK if seq_len % RET_CHUNK == 0 else seq_len
    n_chunks = seq_len // chunk

    def to_chunks(t):
        return t.transpose(0, 2, 1, 3).reshape(bsz, RET_HEADS, n_chunks, chunk, t.shape[-1]).transpose(2, 0, 1, 3, 4)

    def step(state, qkv):
        qc, kc, vc = qkv
        return retention_chunk(state, qc, kc, vc, log_gamma)

    new_state, o = lax.scan(step, state0.astype(f32), (to_chunks(qh), to_chunks(kh), to_chunks(vh)))
    o = o.transpose(1, 2, 0, 3, 4).reshape(bsz, RET_HEADS, seq_len, RET_DV).transpose(0, 2, 1, 3)
    mu = jnp.mean(o, axis=-1, keepdims=True)
    var = jnp.mean(jnp.square(o - mu), axis=-1, keepdims=True)
    o = ((o - mu) * lax.rsqrt(var + EPS)).reshape(bsz, seq_len, RET_V)
    return jax.nn.silu(g.astype(f32)) * o, new_state

def conv_branch(a, buf, pw_b, dw_w, dw_b, ln_g, ln_b):
    f32 = jnp.float32
    a = a + pw_b
    glu = a[..., :CONV_WIDTH] * jax.nn.sigmoid(a[..., CONV_WIDTH:])
    xc = jnp.concatenate([buf.astype(glu.dtype), glu], axis=1)
    y = lax.conv_general_dilated(
        xc, dw_w[:, None, :].astype(xc.dtype), window_strides=(1,), padding="VALID",
        dimension_numbers=("NWC", "WIO", "NWC"), feature_group_count=CONV_WIDTH) + dw_b
    yf = y.astype(f32)
    mu = jnp.mean(yf, axis=-1, keepdims=True)
    var = jnp.mean(jnp.square(yf - mu), axis=-1, keepdims=True)
    yn = (yf - mu) * lax.rsqrt(var + EPS) * ln_g.astype(f32) + ln_b.astype(f32)
    return jax.nn.silu(yn), xc[:, -(CONV_K - 1):]

def mixer_block(h, s5_h0_re, s5_h0_im, ret_s0, conv_buf, pos_offset,
                norm_g, w_in, lam_re, lam_im, log_dt, b_re, b_im, c_re, c_im, d_skip, glu_w, glu_b, s5_proj,
                ret_proj, pw_b, dw_w, dw_b, ln_g, ln_b, conv_proj, w_out):
    f32 = jnp.float32
    u = rmsnorm(h, norm_g)
    z = u @ w_in
    s5_out, s5_re, s5_im = s5_branch(z[..., OFF_S5:OFF_Q], s5_h0_re, s5_h0_im, lam_re, lam_im, log_dt,
                                     b_re, b_im, c_re, c_im, d_skip, glu_w, glu_b)
    ret_out, ret_state = retention_branch(z[..., OFF_Q:OFF_K], z[..., OFF_K:OFF_V], z[..., OFF_V:OFF_G],
                                          z[..., OFF_G:OFF_CONV], ret_s0, pos_offset)
    conv_out, conv_state = conv_branch(z[..., OFF_CONV:OFF_GATE], conv_buf, pw_b, dw_w, dw_b, ln_g, ln_b)
    gates = jax.nn.sigmoid(z[..., OFF_GATE:].astype(f32))
    merged = (gates[..., :D_MODEL] * (s5_out @ s5_proj.astype(f32))
              + gates[..., D_MODEL:2 * D_MODEL] * (ret_out @ ret_proj.astype(f32))
              + gates[..., 2 * D_MODEL:] * (conv_out @ conv_proj.astype(f32)))
    delta = (merged @ w_out.astype(f32)).astype(h.dtype)
    return delta, (s5_re, s5_im, ret_state, conv_state)

def swiglu(x, w_gate, w_up, w_down):
    return (jax.nn.silu(x @ w_gate) * (x @ w_up)) @ w_down

def moe_swiglu(x, router, w_gate, w_up, w_down):
    f32 = jnp.float32
    logits = (x @ router).astype(f32)
    top_v, top_i = lax.top_k(logits, TOP_K)
    top_w = jax.nn.softmax(top_v, axis=-1)
    combine = jnp.sum(jax.nn.one_hot(top_i, N_EXPERTS, dtype=f32) * top_w[..., None], axis=-2)
    out = jnp.zeros(x.shape, f32)
    for e in range(N_EXPERTS):
        out = out + combine[..., e:e + 1] * swiglu(x, w_gate[e], w_up[e], w_down[e]).astype(f32)
    return out.astype(x.dtype)

def setup_inputs(seed: int = 0) -> dict:
    key = jax.random.key(seed)
    keys = iter(jax.random.split(key, 48))
    f32 = jnp.float32

    def nrm(shape, scale):
        return scale * jax.random.normal(next(keys), shape, f32)

    lam_im_base = jnp.pi * jnp.arange(S5_STATE, dtype=f32)
    return {
        "x_prompt": nrm((BATCH, SEQ, D_MODEL), 1.0),
        "x_sample": nrm((DEC_BATCH, DEC_SEQ, D_MODEL), 1.0),
        "state_s5_re": nrm((DEPTH, DEC_BATCH, S5_GROUPS, S5_STATE), 0.1),
        "state_s5_im": nrm((DEPTH, DEC_BATCH, S5_GROUPS, S5_STATE), 0.1),
        "state_ret": nrm((DEPTH, DEC_BATCH, RET_HEADS, RET_DK, RET_DV), 1.0),
        "state_conv": nrm((DEPTH, DEC_BATCH, CONV_K - 1, CONV_WIDTH), 0.5),
        "norm_mix_g": 1.0 + nrm((DEPTH, D_MODEL), 0.02),
        "w_in": nrm((DEPTH, D_MODEL, N_IN), D_MODEL ** -0.5),
        "s5_lambda_re": -0.5 + nrm((DEPTH, S5_GROUPS, S5_STATE), 0.01),
        "s5_lambda_im": lam_im_base + nrm((DEPTH, S5_GROUPS, S5_STATE), 0.01),
        "s5_log_dt": jax.random.uniform(next(keys), (DEPTH, S5_GROUPS), f32, math.log(1e-3), math.log(1e-1)),
        "s5_b_re": nrm((DEPTH, S5_GROUPS, S5_STATE, S5_GROUP), (2.0 * S5_GROUP) ** -0.5),
        "s5_b_im": nrm((DEPTH, S5_GROUPS, S5_STATE, S5_GROUP), (2.0 * S5_GROUP) ** -0.5),
        "s5_c_re": nrm((DEPTH, S5_GROUPS, S5_GROUP, S5_STATE), (2.0 * S5_STATE) ** -0.5),
        "s5_c_im": nrm((DEPTH, S5_GROUPS, S5_GROUP, S5_STATE), (2.0 * S5_STATE) ** -0.5),
        "s5_d": nrm((DEPTH, S5_WIDTH), 1.0),
        "s5_glu_w": nrm((DEPTH, S5_WIDTH, S5_WIDTH), S5_WIDTH ** -0.5),
        "s5_glu_b": nrm((DEPTH, S5_WIDTH), 0.01),
        "s5_proj": nrm((DEPTH, S5_WIDTH, D_MODEL), S5_WIDTH ** -0.5),
        "ret_proj": nrm((DEPTH, RET_V, D_MODEL), RET_V ** -0.5),
        "conv_pw_b": nrm((DEPTH, 2 * CONV_WIDTH), 0.01),
        "conv_dw_w": nrm((DEPTH, CONV_K, CONV_WIDTH), CONV_K ** -0.5),
        "conv_dw_b": nrm((DEPTH, CONV_WIDTH), 0.01),
        "conv_ln_g": 1.0 + nrm((DEPTH, CONV_WIDTH), 0.02),
        "conv_ln_b": nrm((DEPTH, CONV_WIDTH), 0.01),
        "conv_proj": nrm((DEPTH, CONV_WIDTH, D_MODEL), CONV_WIDTH ** -0.5),
        "w_out": nrm((DEPTH, D_MODEL, D_MODEL), D_MODEL ** -0.5),
        "norm_ffn_g": 1.0 + nrm((DEPTH, D_MODEL), 0.02),
        "ffn_w_gate": nrm((N_DENSE, D_MODEL, D_FF), D_MODEL ** -0.5),
        "ffn_w_up": nrm((N_DENSE, D_MODEL, D_FF), D_MODEL ** -0.5),
        "ffn_w_down": nrm((N_DENSE, D_FF, D_MODEL), D_FF ** -0.5),
        "moe_router": nrm((N_MOE, D_MODEL, N_EXPERTS), D_MODEL ** -0.5),
        "moe_w_gate": nrm((N_MOE, N_EXPERTS, D_MODEL, D_FF_EXPERT), D_MODEL ** -0.5),
        "moe_w_up": nrm((N_MOE, N_EXPERTS, D_MODEL, D_FF_EXPERT), D_MODEL ** -0.5),
        "moe_w_down": nrm((N_MOE, N_EXPERTS, D_FF_EXPERT, D_MODEL), D_FF_EXPERT ** -0.5),
        "norm_final_g": 1.0 + nrm((D_MODEL,), 0.02),
    }

def reference(x_prompt, x_sample, state_s5_re, state_s5_im, state_ret, state_conv,
              norm_mix_g, w_in, s5_lambda_re, s5_lambda_im, s5_log_dt, s5_b_re, s5_b_im, s5_c_re, s5_c_im,
              s5_d, s5_glu_w, s5_glu_b, s5_proj, ret_proj, conv_pw_b, conv_dw_w, conv_dw_b, conv_ln_g, conv_ln_b,
              conv_proj, w_out, norm_ffn_g, ffn_w_gate, ffn_w_up, ffn_w_down,
              moe_router, moe_w_gate, moe_w_up, moe_w_down, norm_final_g):
    f32 = jnp.float32
    bp = x_prompt.shape[0]
    zero_s5 = jnp.zeros((bp, S5_GROUPS, S5_STATE), f32)
    zero_ret = jnp.zeros((bp, RET_HEADS, RET_DK, RET_DV), f32)
    zero_conv = jnp.zeros((bp, CONV_K - 1, CONV_WIDTH), x_prompt.dtype)
    hp = x_prompt
    hs = x_sample
    p_re_l, p_im_l, p_ret_l, p_conv_l = [], [], [], []
    s_re_l, s_im_l, s_ret_l, s_conv_l = [], [], [], []
    for l in range(DEPTH):
        layer_params = (norm_mix_g[l], w_in[l], s5_lambda_re[l], s5_lambda_im[l], s5_log_dt[l],
                        s5_b_re[l], s5_b_im[l], s5_c_re[l], s5_c_im[l], s5_d[l], s5_glu_w[l], s5_glu_b[l],
                        s5_proj[l], ret_proj[l], conv_pw_b[l], conv_dw_w[l], conv_dw_b[l], conv_ln_g[l],
                        conv_ln_b[l], conv_proj[l], w_out[l])
        dp, (p_re, p_im, p_ret, p_conv) = mixer_block(hp, zero_s5, zero_s5, zero_ret, zero_conv, 0, *layer_params)
        ds, (s_re, s_im, s_ret, s_conv) = mixer_block(hs, state_s5_re[l], state_s5_im[l], state_ret[l],
                                                      state_conv[l], PAST_LEN, *layer_params)
        hp = hp + dp
        hs = hs + ds
        up = rmsnorm(hp, norm_ffn_g[l])
        us = rmsnorm(hs, norm_ffn_g[l])
        j = l // 2
        if l % 2 == 0:
            hp = hp + swiglu(up, ffn_w_gate[j], ffn_w_up[j], ffn_w_down[j])
            hs = hs + swiglu(us, ffn_w_gate[j], ffn_w_up[j], ffn_w_down[j])
        else:
            hp = hp + moe_swiglu(up, moe_router[j], moe_w_gate[j], moe_w_up[j], moe_w_down[j])
            hs = hs + moe_swiglu(us, moe_router[j], moe_w_gate[j], moe_w_up[j], moe_w_down[j])
        p_re_l.append(p_re)
        p_im_l.append(p_im)
        p_ret_l.append(p_ret)
        p_conv_l.append(p_conv)
        s_re_l.append(s_re)
        s_im_l.append(s_im)
        s_ret_l.append(s_ret)
        s_conv_l.append(s_conv)
    y_prompt = rmsnorm(hp, norm_final_g)
    y_sample = rmsnorm(hs, norm_final_g)
    s5_re_prompt = jnp.stack(p_re_l)
    s5_im_prompt = jnp.stack(p_im_l)
    ret_prompt = jnp.stack(p_ret_l)
    conv_prompt = jnp.stack(p_conv_l)
    s5_re_sample = jnp.stack(s_re_l)
    s5_im_sample = jnp.stack(s_im_l)
    ret_sample = jnp.stack(s_ret_l)
    conv_sample = jnp.stack(s_conv_l)
    return (y_prompt, y_sample, s5_re_prompt, s5_im_prompt, ret_prompt, conv_prompt,
            s5_re_sample, s5_im_sample, ret_sample, conv_sample)


_drawn_inputs = setup_inputs


def setup_inputs(seed=0):
    import zlib

    import numpy as np

    out = dict(_drawn_inputs(seed))
    spreads = {}
    factors = {'s5_lambda_re': 55.382,
     's5_c_im': 3.031,
     's5_glu_b': 22.293,
     'conv_pw_b': 3.828,
     'conv_ln_b': 3.063,
     'norm_final_g': 25.426,
     's5_c_re': 3.336}
    for name, (base, spread) in spreads.items():
        noise = np.random.default_rng([zlib.crc32(name.encode()), seed]).standard_normal(out[name].shape)
        drawn = base * np.exp(spread * noise) if base else spread * noise
        out[name] = jnp.asarray(drawn.astype(out[name].dtype))
    for name, factor in factors.items():
        out[name] = (out[name] * factor).astype(out[name].dtype)
    return out
```

```python
import numpy as np

P = 128
D = 1024
KD = D // P
SEQ = 256
NS = 8
T = SEQ + NS
DEPTH = 2
G = 32
GP = 16
GJ = G // 2
S = 8
NC = SEQ // S
HEADS = 4
DV = 256
TAPS = 31
F_DENSE = 2816 // P
F_EXP = 3584 // P
NEXP = 8
CAP = 112
EPS = 1e-6
CH = 16
NBANK = 8
WIDE = 512
E_TILES = 3584 // WIDE
GU = 4 * E_TILES
DN = F_EXP // 2
E_CHUNKS = GU + DN
RING = 4
MRING = 7
HRING = 6
AHEAD = 4
UT = [(0, 128), (128, 128), (256, 8)]
BIG = 4096.0

V_GM, V_GF, V_PWB, V_DWW, V_DWB, V_LNG, V_LNB, V_GLB = 0, 8, 16, 24, 148, 152, 156, 160
V_L = 164
V_FIN = DEPTH * V_L
NV = V_FIN + 8


def tile_order():
    o = []
    for l in range(DEPTH):
        def add(name, n, blocks=0):
            for i in range(n):
                o.append(((l, name, i), blocks))
        add("ms1", 1)
        for name, n in (("cb", 4), ("ca", 4), ("zs", 4), ("q", 4), ("k", 4), ("v", 8)):
            add(name, n, KD)
        add("vt", 4); add("vs", 2); add("kt", 2); add("ks", 1)
        add("win", 8); add("kk", 8)
        for h in range(HEADS):
            o += [((l, "sc", h), 0), ((l, "ou", h), 0), ((l, "st", h), 0)]
        add("si", 4); add("cm", 1); add("cv", 1)
        for d in range(KD):
            o += [((l, "gc", d), KD), ((l, "pc", d), 4)]
            o += [((l, "oa", d), 0), ((l, "ob", d), 0), ((l, "os", d), 0)]
        add("gm", 4); add("gv", 4); add("y", 4)
        add("gg", 8, KD)
        for d in range(KD):
            o += [((l, "gr", d), KD), ((l, "pr", d), KD)]
        add("gl", 4, 4)
        for d in range(KD):
            o += [((l, "gs", d), KD), ((l, "ps", d), 4)]
        add("wo", 8, KD)
        add("ms2", 1)
        if l == 0:
            for f in range(F_DENSE):
                o += [((l, "fg", f), KD), ((l, "fu", f), KD)]
            add("dn", 8, F_DENSE)
    l = DEPTH - 1
    o += [((l, "tt", i), 0) for i in range(6)]
    o += [((l, "lg", i), 0) for i in range(3)]
    o += [((l, "po", 0), 0)]
    return o


def tile_counts():
    place, done, chunk = {}, {}, []
    n = b = 0
    for i, (key, blocks) in enumerate(tile_order()):
        place[key] = i
        for x in range(blocks):
            b += 1
            if b % CH == 0:
                if x < blocks - 1:
                    n += 1
                    chunk.append(n)
                else:
                    chunk.append(n + 1)
        n += 1
        done[key] = n
    assert b % CH == 0
    return place, done, chunk, n


def build(nc, a):
    import concourse.bass as bass
    from concourse import mybir
    from contextlib import ExitStack

    F = mybir.dt.float32
    F32R = mybir.dt.float32r
    I32 = mybir.dt.int32
    U32 = mybir.dt.uint32
    ACT = mybir.ActivationFunctionType
    ALU = mybir.AluOpType
    AX = mybir.AxisListType.X
    PLACE, DONE, CHUNK_DONE, MM_BASE = tile_counts()
    N_CHUNKS = len(CHUNK_DONE)

    with ExitStack() as ctx:
        start_of = {}

        def sb(name, shape, dt=F):
            start_of[name] = -(-nc.sbuf_base // 32) * 32
            return ctx.enter_context(nc.sbuf_tensor(name, shape, dt))

        def parts_of(name, width):
            return nc.alloc_sbuf_tensor_at(name + "_parts", [P, width], F32R, offset=start_of[name])

        def sem(name):
            return ctx.enter_context(nc.semaphore(name))

        xT = sb("xT", [P, KD, T])
        uT = sb("uT", [P, KD, T])
        ring = sb("ring", [P, RING, 2048])
        s5m = sb("s5m", [P, 15648])
        zone = sb("zone", [P, 10520])
        work = sb("work", [P, 7784])
        sq = sb("sq", [P, 1056])
        rstd = sb("rstd", [P, 2, T])
        gate = sb("gate", [P, 2, T])
        tmp = sb("tmp", [P, 2, T])
        rope = sb("rope", [P, 4, T])
        decay = sb("decay", [P, HEADS, SEQ])
        kdec = sb("kdec", [P, 2, HEADS])
        ident = sb("ident", [P, P])
        tri = sb("tri", [P, P])
        ones = sb("ones", [P, P])
        iota = sb("iota", [P, CAP])
        vecs = sb("vecs", [P, NV])
        eps = sb("eps", [P, 1])
        lam = sb("lam", [P, 3, DEPTH * GJ])
        lw = sb("lw", [P, 16, DEPTH * GJ])
        dskip = sb("dskip", [GP, DEPTH, G])
        l8 = sb("l8", [P, 4, GJ])
        rec = sb("rec", [P, 3, 2, GJ])
        qs = sb("qs", [P, HEADS, NS])
        router = sb("router", [P, KD, NEXP])

        toep = s5m[:, 0:4096].rearrange("p (g x) -> p g x", g=G)
        gb = s5m[:, 0:4096].rearrange("p (j r s q) -> p j r s q", j=GJ, r=2, s=S)
        gb2 = s5m[:, 0:4096]
        winT = s5m[:, 4096:8192]
        clr = s5m[:, 8192:10496].rearrange("p (j x) -> p j x", j=GJ)
        cli = s5m[:, 10496:12800].rearrange("p (j x) -> p j x", j=GJ)
        xin = s5m[:, 12800:14336].rearrange("p (g x) -> p g x", g=G)
        hst = s5m[:, 14336:15648].rearrange("p (r j c) -> p r j c", r=2, j=GJ)
        sigb = zone[:, 0:1056].rearrange("p (m t) -> p m t", m=4)
        xc = zone[:, 1056:2200].rearrange("p (m t) -> p m t", m=4)
        yg = zone[:, 1056:2112].rearrange("p (m t) -> p m t", m=4)
        xs = zone[:, 2200:3192].rearrange("p (m b k) -> p m b k", m=4, b=NS)
        cT = zone[:, 3192:4248].rearrange("p (m t) -> p m t", m=4)
        qT = zone[:, 4248:5304].rearrange("p (h t) -> p h t", h=HEADS)
        kT = zone[:, 5304:6360].rearrange("p (h t) -> p h t", h=HEADS)
        mT = zone[:, 4248:6360].rearrange("p (m t) -> p m t", m=KD)
        vT = zone[:, 6360:8472].rearrange("p (m t) -> p m t", m=KD)
        vtok = zone[:, 8472:10520].rearrange("p (i x) -> p i x", i=2)
        ys = zone[:, 8472:9752].rearrange("p (g c) -> p g c", g=G)
        hT = zone[:, 0:F_DENSE * T].rearrange("p (f t) -> p f t", f=F_DENSE)
        kd = work[:, 0:1024].rearrange("p (i x) -> p i x", i=2)
        pt = work[:, 1024:1792].rearrange("p (b x) -> p b x", b=2)
        si = work[:, 0:1536].rearrange("p (r j c) -> p r j c", r=2, j=GJ)
        kst = work[:, 1792:2304]
        kmask = work[:, 2304:3328].rearrange("p (b x) -> p b x", b=2)
        vst = work[:, 3328:4352]
        sring = work[:, 4352:6400].rearrange("p (b h x) -> p b h x", b=2, h=HEADS)
        hnew = work[:, 7424:7680].rearrange("p (r j b) -> p r j b", r=2, j=GJ)
        stst = work[:, 6400:7424].rearrange("p (h x) -> p h x", h=HEADS)
        bc = work[:, 0:1024].rearrange("p (w j q) -> p w j q", w=4, j=GJ)
        bb = work[:, 1024:1536].rearrange("p (r j q) -> p r j q", r=2, j=GJ)
        pa = work[:, 1536:1824].rearrange("p (r k j) -> p r k j", r=2, k=9)
        pd = work[:, 1824:2080].rearrange("p (r k j) -> p r k j", r=2, k=8)
        pw = work[:, 2080:2208].rearrange("p (r k j) -> p r k j", r=2, k=4)
        pt1 = work[:, 2304:4608]
        dd = work[0:GP, 4608:5120].rearrange("p (g q) -> p g q", g=G)
        utok = work[:, 0:3072].rearrange("p (i x) -> p i x", i=3)
        sel = work[:, 3072:3408].rearrange("p (i c) -> p i c", i=3)
        selw = work[:, 3408:3744].rearrange("p (i c) -> p i c", i=3)
        selT = work[:, 3744:4008]
        ytok = work[:, 4904:5928]
        hm = work[:, 5928:6952].rearrange("p (b x) -> p b x", b=2)
        rt = work[:, 7144:7624].rearrange("p (w i e) -> p w i e", i=3, e=8)
        rti = sq[:, 0:24].bitcast(U32).rearrange("p (i e) -> p i e", i=3)
        items_t = sq[:, 24:25].bitcast(I32)
        slotx = work[:, 7624:7699].rearrange("p (i c) -> p i c", i=3)
        combx = work[:, 7699:7774].rearrange("p (i c) -> p i c", i=3)
        cur = work[:, 7774:7783].rearrange("p (w i) -> p w i", w=3)
        hfin = sb("hfin", [P, 2, GJ])
        HE = F_EXP * CAP

        s5m_parts = parts_of("s5m", 15648)
        ring_parts = parts_of("ring", RING * 2048)
        zone_parts = parts_of("zone", 10520)
        work_parts = parts_of("work", 7784)
        decay_parts = parts_of("decay", HEADS * SEQ)
        xg_hi = work_parts[:, 4008:4904].rearrange("p (k c) -> p k c", k=KD)
        xg_lo = decay_parts[:, 0:KD * CAP].rearrange("p (k c) -> p k c", k=KD)
        hE_hi = zone_parts[:, 0:HE].rearrange("p (f c) -> p f c", f=F_EXP)
        hE_lo = zone_parts[:, HE:2 * HE].rearrange("p (f c) -> p f c", f=F_EXP)

        def slot(c, of):
            s = c % MRING
            return of[:, s * 2048:(s + 1) * 2048]

        def high_slot(c):
            s = c % HRING
            if s < RING:
                return ring_parts[:, s * 2048:(s + 1) * 2048]
            o = 2 * HE + (s - RING) * 2048
            return zone_parts[:, o:o + 2048]

        def f32(ap):
            return ap.bitcast(F)

        bank = [ctx.enter_context(nc.psum_tensor(f"bank{b}", [P, 512], F)) for b in range(NBANK)]

        zscr = nc.dram_tensor("zscr", [G * GP, T], F, kind="Internal").ap()
        yscr = nc.dram_tensor("yscr", [G * GP, T], F, kind="Internal").ap()
        kscr = nc.dram_tensor("kscr", [G, GP, 2 * P], F, kind="Internal").ap()

        consts_in = sem("consts_in")
        ones_set = sem("ones_set")
        loaded = [sem(f"loaded{s}") for s in range(RING)]
        mloaded = [sem(f"mloaded{s}") for s in range(MRING)]
        mm_done = sem("mm_done")
        evicted = [sem(f"bank_evicted{b}") for b in range(NBANK)]
        act_order = sem("act_order")
        dve_order = sem("dve_order")
        pool_order = sem("pool_order")
        squares = sem("squares_done")
        std_done = sem("std_done")
        u_ready = sem("u_ready")
        lam_ready = sem("lam_ready")
        lam_act = sem("lam_act")
        conv_step = sem("conv_step")
        conv_done = sem("conv_done")
        conv_state_in = sem("conv_state_in")
        conv_state_out = sem("conv_state_out")
        conv_act = sem("conv_act")
        pt_ready = sem("pt_ready")
        l8_ready = sem("l8_ready")
        gb_ready = sem("gb_ready")
        kmat_ready = sem("kmat_ready")
        kscr_out = sem("kscr_out")
        toep_in = sem("toep_in")
        bc_in = sem("bc_in")
        zero_out = sem("zero_out")
        zscr_out = sem("zscr_out")
        xin_in = sem("xin_in")
        h0_in = sem("h0_in")
        h_ready = sem("h_ready")
        hstate_out = sem("hstate_out")
        yscr_out = sem("yscr_out")
        y_in = sem("y_in")
        kmask_ready = sem("kmask_ready")
        s_in = [sem(f"s_in{b}") for b in range(2)]
        s_out = [sem(f"s_out{b}") for b in range(2)]
        st_out = sem("st_out")
        qs_ready = sem("qs_ready")
        gn_ready = sem("gn_ready")
        cn_ready = sem("cn_ready")
        gated = sem("gated")
        gelu_done = sem("gelu_done")
        glu_done = sem("glu_done")
        merged = sem("merged")
        ff_gate = sem("ff_gate")
        route_act = sem("route_act")
        route_ready = sem("route_ready")
        items_ready = sem("items_ready")
        sel_ready = sem("sel_ready")
        cur_ready = sem("cur_ready")
        misc_done = sem("misc_done")
        high_done = sem("high_done")
        low_done = sem("low_done")
        eg_done = sem("eg_done")
        hidden_high = sem("hidden_high")
        gathered_high = sem("gathered_high")
        y_out = sem("y_out")
        xin_zero = sem("xin_zero")
        x_final = sem("x_final")

        def at(key):
            return bank[PLACE[key] % NBANK]

        def out_of(key):
            return evicted[PLACE[key] % NBANK], PLACE[key] // NBANK + 1

        def freed(key):
            return evicted[PLACE[key] % NBANK]

        def vec(l, col, m):
            c = l * V_L + col + m
            return vecs[:, c:c + 1]

        BASE = [sum(1 for i in range(len(PLACE)) if i % NBANK == b) + (b in (1, 3)) for b in range(NBANK)]
        USES = [4 + 2, 3 + 1, 4 + 2, 3 + 1, 4 + 2, 3 + 1 + 2, 1, 1]
        SCATTER = (0, 2, 4, 5)
        SCATTER_USE = (4, 4, 4, 4)
        M_ONEHOT, M_GATHER, M_SCATTER = E_TILES, E_TILES + 1, E_TILES + 3
        MISC = M_SCATTER + KD
        MISC0 = 2
        TURNS = E_CHUNKS // MRING

        block = ctx.enter_context(nc.Block())

        @block.sync
        def _(sp):
            loads = [(xT[:, :, :], a["xT"]), (vecs[:, :], a["vecs"]), (lam[:, :, :], a["lam"]),
                     (rope[:, :, :], a["rope"]), (decay[:, :, :], a["decay"]), (kdec[:, :, :], a["kdec"]),
                     (ident[:, :], a["ident"]), (tri[:, :], a["tri"]), (iota[:, :], a["iota"]),
                     (dskip[:, :, :], a["dskip"]), (router[:, :, :], a["router"])]
            for dst, src in loads:
                sp.dma_start(dst, src).then_inc(consts_in, 16)

            for n in range(RING):
                sp.dma_start(ring[:, n, :], a["weights"][n]).then_inc(loaded[n], 16)
            for n in range(RING, N_CHUNKS):
                sp.wait_ge(mm_done, CHUNK_DONE[n - RING])
                sp.dma_start(ring[:, n % RING, :], a["weights"][n]).then_inc(loaded[n % RING], 16)

            sp.wait_ge(mm_done, DONE[(DEPTH - 1, "y", 3)])
            sp.wait_ge(hstate_out, 32 * DEPTH)
            for s in range(MRING):
                sp.dma_start(slot(s, s5m), a["experts"][s]).then_inc(mloaded[s], 16)
            sp.wait_ge(items_ready, 1)
            items = sp.value_load(items_t[0:1, 0:1], min_val=NEXP, max_val=3 * NEXP)
            with sp.Fori(0, items * TURNS - 1) as q:
                for s in range(MRING):
                    sp.wait_ge(mm_done, q * MRING + MM_BASE + s + 1)
                    row = ((q + 1) % (NEXP * TURNS)) * MRING + s
                    sp.dma_start(slot(s, s5m), a["experts"][bass.ds(row, 1)].rearrange("o p x -> (o p) x")
                                 ).then_inc(mloaded[s], 16)

            sp.wait_ge(x_final, 1)
            sp.dma_start(a["y"], uT[:, :, :]).then_inc(y_out, 16)
            sp.wait_ge(y_out, 16)

        @block.tensor
        def _(pe):
            state = {"tile": 0, "block": 0}

            def open_tile(key):
                n = state["tile"]
                assert PLACE[key] == n, (key, n)
                state["tile"] += 1
                if n >= NBANK:
                    pe.wait_ge(evicted[n % NBANK], n // NBANK)
                return bank[n % NBANK]

            def weight_tile(key, rhs, n_blocks, width=T):
                out = open_tile(key)
                for k in range(n_blocks):
                    b = state["block"]
                    c = b // CH
                    if b % CH == 0:
                        pe.wait_ge(loaded[c % RING], 16 * (c // RING + 1))
                    x = b % CH
                    mm = pe.matmul(out[:, 0:width], ring[:, c % RING, x * P:(x + 1) * P], rhs(k),
                                   start=(k == 0), stop=(k == n_blocks - 1))
                    state["block"] += 1
                    if (b + 1) % CH == 0 and k < n_blocks - 1:
                        mm.then_inc(mm_done, 1)
                mm.then_inc(mm_done, 1)

            def sum_tile(key, parts, n):
                out = open_tile(key)
                for i in range(n):
                    mm = pe.matmul(out[:, 0:T], ones[:, :], parts(i), start=(i == 0), stop=(i == n - 1))
                mm.then_inc(mm_done, 1)

            def u_block(k):
                return uT[:, k, :]

            pe.wait_ge(consts_in, 16 * 11)
            pe.wait_ge(ones_set, 2)
            for l in range(DEPTH):
                pe.wait_ge(squares, 7 * l + 1)
                sum_tile((l, "ms1", 0), lambda k: uT[:, k, :], KD)
                pe.wait_ge(u_ready, 2 * l + 1)
                for name, n in (("cb", 4), ("ca", 4), ("zs", 4), ("q", 4), ("k", 4), ("v", 8)):
                    for m in range(n):
                        weight_tile((l, name, m), u_block, KD)
                for i in range(4):
                    it, half = i // 2, i % 2
                    pe.wait_ge(*out_of((l, "v", 4 * half + 3)))
                    out = open_tile((l, "vt", i))
                    for m in range(4):
                        mm = pe.transpose(out[:, m * P:(m + 1) * P], vT[:, 4 * half + m, it * P:(it + 1) * P], ident[:, :])
                    mm.then_inc(mm_done, 1)
                for half in range(2):
                    out = open_tile((l, "vs", half))
                    for m in range(4):
                        mm = pe.transpose(out[0:NS, m * P:(m + 1) * P], vT[:, 4 * half + m, SEQ:T], ident[:, :])
                    mm.then_inc(mm_done, 1)
                pe.wait_ge(*out_of((l, "k", 3)))
                pe.wait_ge(qs_ready, l + 1)
                for i in range(2):
                    out = open_tile((l, "kt", i))
                    for h in range(HEADS):
                        mm = pe.transpose(out[:, h * P:(h + 1) * P], kT[:, h, i * P:(i + 1) * P], ident[:, :])
                    mm.then_inc(mm_done, 1)
                out = open_tile((l, "ks", 0))
                for h in range(HEADS):
                    mm = pe.transpose(out[0:NS, h * P:(h + 1) * P], kT[:, h, SEQ:T], ident[:, :])
                mm.then_inc(mm_done, 1)
                pe.wait_ge(gb_ready, l + 1)
                for i in range(8):
                    out = open_tile((l, "win", i))
                    for x in range(4):
                        c = (4 * i + x) * P
                        mm = pe.transpose(out[:, x * P:(x + 1) * P], gb2[:, c:c + P], ident[:, :])
                    mm.then_inc(mm_done, 1)
                for i in range(8):
                    out = open_tile((l, "kk", i))
                    g2 = i // 4
                    lo, hi = 64 * g2, 64 * g2 + 64
                    for x in range(4):
                        j = 4 * (i % 4) + x
                        pe.matmul(out[0:GP, x * P:(x + 1) * P], bb[lo:hi, 0, j, :], clr[lo:hi, j, 0:P],
                                  start=True, stop=False)
                        mm = pe.matmul(out[0:GP, x * P:(x + 1) * P], bb[lo:hi, 1, j, :], cli[lo:hi, j, 0:P],
                                       start=False, stop=True)
                    mm.then_inc(mm_done, 1)
                pe.wait_ge(*out_of((l, "kt", 1)))
                pe.wait_ge(*out_of((l, "vt", 3)))
                pe.wait_ge(*out_of((l, "vt", 2)))
                pe.wait_ge(*out_of((l, "vt", 1)))
                pe.wait_ge(*out_of((l, "vt", 0)))
                pe.wait_ge(*out_of((l, "kt", 0)))
                for h in range(HEADS):
                    out = open_tile((l, "sc", h))
                    pe.matmul(out[:, 0:SEQ], kT[:, h, 0:P], qT[:, h, 0:SEQ], start=True, stop=True)
                    pe.matmul(out[:, SEQ:SEQ + P], kT[:, h, P:SEQ], qT[:, h, P:SEQ], start=True, stop=True
                              ).then_inc(mm_done, 1)
                    out = open_tile((l, "ou", h))
                    pe.wait_ge(*out_of((l, "sc", h)))
                    for half in range(2):
                        c = h * DV + half * P
                        pe.matmul(out[:, half * SEQ:(half + 1) * SEQ], vtok[:, 0, c:c + P], pt[:, h % 2, 0:SEQ],
                                  start=True, stop=False)
                        mm = pe.matmul(out[:, half * SEQ + P:(half + 1) * SEQ], vtok[:, 1, c:c + P],
                                       pt[:, h % 2, SEQ:SEQ + P], start=False, stop=True)
                    mm.then_inc(mm_done, 1)
                    out = open_tile((l, "st", h))
                    for i in range(2):
                        mm = pe.matmul(out[:, 0:DV], kd[:, i, h * P:(h + 1) * P], vtok[:, i, h * DV:(h + 1) * DV],
                                       start=(i == 0), stop=(i == 1))
                    mm.then_inc(mm_done, 1)
                pe.wait_ge(xin_in, 160 * (l + 1))
                for i in range(8):
                    pe.wait_ge(*out_of((l, "win", i)))
                for i in range(4):
                    out = open_tile((l, "si", i))
                    for x in range(8):
                        j, ri = 4 * i + x // 2, x % 2
                        for g2 in range(2):
                            c = (2 * j + ri) * P + 64 * g2
                            mm = pe.matmul(out[64 * g2:64 * g2 + 64, x * 48:(x + 1) * 48], winT[:, c:c + 64],
                                           xin[:, g2 * GJ + j, :], start=True, stop=True)
                    mm.then_inc(mm_done, 1)
                pe.wait_ge(conv_done, l + 1)
                sum_tile((l, "cm", 0), lambda m: cT[:, m, :], 4)
                pe.wait_ge(squares, 7 * l + 2)
                sum_tile((l, "cv", 0), lambda m: sq[:, m * T:(m + 1) * T], 4)
                pe.wait_ge(conv_act, l + 1)
                for b in range(NS):
                    weight_tile((l, "gc", b), u_block, KD)
                    weight_tile((l, "pc", b), lambda k: cT[:, k, :], 4)
                    pe.wait_ge(kmask_ready, NS * l + b + 1)
                    for half, name in ((0, "oa"), (1, "ob")):
                        out = open_tile((l, name, b))
                        for x in range(2):
                            h = 2 * half + x
                            mm = pe.matmul(out[:, x * DV:(x + 1) * DV], kmask[0:NS, b % 2, h * P:(h + 1) * P],
                                           vst[0:NS, h * DV:(h + 1) * DV], start=True, stop=True)
                        mm.then_inc(mm_done, 1)
                    out = open_tile((l, "os", b))
                    pe.wait_ge(*out_of((l, "oa", b)))
                    pe.wait_ge(*out_of((l, "ob", b)))
                    for x in range(KD):
                        h, half = x // 2, x % 2
                        mm = pe.matmul(out[:, x:x + 1], sring[:, b % 2, h, half * P:(half + 1) * P],
                                       qs[:, h, b:b + 1], start=True, stop=True)
                    mm.then_inc(mm_done, 1)
                for h in range(HEADS):
                    pe.wait_ge(*out_of((l, "ou", h)))
                for b in range(NS):
                    pe.wait_ge(*out_of((l, "os", b)))
                for h in range(HEADS):
                    sum_tile((l, "gm", h), lambda x: vT[:, 2 * h + x, :], 2)
                for h in range(HEADS):
                    pe.wait_ge(squares, 7 * l + 3 + h)
                    c = (h % 2) * 2 * T
                    sum_tile((l, "gv", h), lambda x: sq[:, c + x * T:c + (x + 1) * T], 2)
                pe.wait_ge(h_ready, l + 1)
                pe.wait_ge(toep_in, 128 * (l + 1))
                for i in range(4):
                    out = open_tile((l, "y", i))
                    g2 = i // 2
                    lo, hi = 64 * g2, 64 * g2 + 64
                    for x in range(8):
                        g = 8 * i + x
                        j = g % GJ
                        o = out[:, x * 40:(x + 1) * 40]
                        pe.matmul(o, toep[:, g, :], xin[:, g, 0:40], start=True, stop=False)
                        pe.matmul(o, clr[lo:hi, j, GP:GP + P], hst[lo:hi, 0, j, 0:40], start=False, stop=False)
                        mm = pe.matmul(o, cli[lo:hi, j, GP:GP + P], hst[lo:hi, 1, j, 0:40], start=False, stop=True)
                    mm.then_inc(mm_done, 1)
                for m in range(KD):
                    weight_tile((l, "gg", m), u_block, KD)
                pe.wait_ge(gated, KD * (l + 1))
                for d in range(KD):
                    weight_tile((l, "gr", d), u_block, KD)
                    weight_tile((l, "pr", d), lambda k: vT[:, k, :], KD)
                pe.wait_ge(gelu_done, l + 1)
                for m in range(4):
                    weight_tile((l, "gl", m), lambda k: yg[:, k, :], 4)
                for d in range(KD):
                    weight_tile((l, "gs", d), u_block, KD)
                    if d == 0:
                        pe.wait_ge(glu_done, 4 * (l + 1))
                    weight_tile((l, "ps", d), lambda k: sigb[:, k, :], 4)
                pe.wait_ge(merged, 16 * (l + 1))
                for d in range(KD):
                    weight_tile((l, "wo", d), lambda k: mT[:, k, :], KD)
                pe.wait_ge(squares, 7 * l + 7)
                sum_tile((l, "ms2", 0), lambda k: uT[:, k, :], KD)
                pe.wait_ge(u_ready, 2 * l + 2)
                if l == 0:
                    for f in range(F_DENSE):
                        weight_tile((l, "fg", f), u_block, KD)
                        weight_tile((l, "fu", f), u_block, KD)
                    for f in range(F_DENSE - 4, F_DENSE):
                        pe.wait_ge(*out_of((l, "fu", f)))
                    for d in range(KD):
                        weight_tile((l, "dn", d), lambda k: hT[:, k, :], F_DENSE)

            l = DEPTH - 1
            for i in range(6):
                t, half = i // 2, i % 2
                lo, n = UT[t]
                out = open_tile((l, "tt", i))
                for k in range(4):
                    mm = pe.transpose(out[0:n, k * P:(k + 1) * P], uT[:, 4 * half + k, lo:lo + n], ident[:, :])
                mm.then_inc(mm_done, 1)
            for i in range(3):
                lo, n = UT[i]
                out = open_tile((l, "lg", i))
                for k in range(KD):
                    mm = pe.matmul(out[0:n, 0:NEXP], uT[:, k, lo:lo + n], router[:, k, :], start=(k == 0), stop=(k == KD - 1))
                mm.then_inc(mm_done, 1)
            pe.wait_ge(route_ready, 1)
            out = open_tile((l, "po", 0))
            for i in range(3):
                n = UT[i][1]
                for x in range(i + 1):
                    k = UT[x][1]
                    left = tri[0:k, 0:n] if x == i else ones[0:k, 0:n]
                    pe.matmul(out[0:n, 8 * i:8 * i + 8], left, rt[0:k, 6, x, :], start=(x == 0), stop=(x == i))
            for x in range(3):
                k = UT[x][1]
                mm = pe.matmul(out[:, 24:32], ones[0:k, :], rt[0:k, 6, x, :], start=(x == 0), stop=(x == 2))
            mm.then_inc(mm_done, 1)

            for i in range(6):
                pe.wait_ge(*out_of((l, "tt", i)))

            def gather():
                for half in range(2):
                    for x in range(4):
                        for i in range(3):
                            n = UT[i][1]
                            c = (4 * half + x) * P
                            mm = pe.matmul(bank[1 + 2 * half][:, x * CAP:(x + 1) * CAP], utok[0:n, i, c:c + P],
                                           sel[0:n, i, :], start=(i == 0), stop=(i == 2))
                    mm.then_inc(misc_done, 1)

            def split_product(out, left, left_lo, right, right_lo, first, last):
                pe.matmul(out, left, right_lo, start=first, stop=False)
                pe.matmul(out, left_lo, right, start=False, stop=False)
                return pe.matmul(out, left, right, start=False, stop=last)

            pe.wait_ge(sel_ready, 1)
            for b in (1, 3):
                pe.wait_ge(evicted[b], BASE[b] - 1)
            gather()
            pe.wait_ge(items_ready, 1)
            items = pe.value_load(items_t[0:1, 0:1], min_val=NEXP, max_val=3 * NEXP)
            with pe.Fori(0, items) as it:

                def bank_free(b, use):
                    pe.wait_ge(evicted[b], it * USES[b] + BASE[b] + use)

                def expert_tile(b, t, c):
                    bank_free(b, t // 2)
                    for k in range(KD):
                        if k % 4 == 0:
                            pe.wait_ge(low_done, it * E_CHUNKS + c + k // 4 + 1)
                        w = slice((k % 4) * WIDE, (k % 4 + 1) * WIDE)
                        mm = split_product(bank[b][0:CAP, :], xg_hi[:, k, :], xg_lo[:, k, :], high_slot(c + k // 4)[:, w],
                                           slot(c + k // 4, s5m_parts)[:, w], k == 0, k == KD - 1)
                        if k % 4 == 3:
                            mm.then_inc(mm_done, 1)

                def hidden_transpose(t):
                    b = 4 + t % 2
                    bank_free(2 + t % 2, t // 2 + 1)
                    bank_free(b, t // 2)
                    for x in range(4):
                        mm = pe.transpose(bank[b][:, x * CAP:(x + 1) * CAP], hm[0:CAP, t % 2, x * P:(x + 1) * P],
                                          ident[0:CAP, 0:CAP])
                    mm.then_inc(misc_done, 1)

                for b in (1, 3):
                    bank_free(b, 0)
                for t in range(E_TILES):
                    expert_tile(t % 2, t, 4 * t)
                    if t > 0:
                        hidden_transpose(t - 1)
                    expert_tile(2 + t % 2, t, 4 * t + 2)
                for b in (6, 7):
                    bank_free(b, 0)
                for j in range(DN):
                    if j == 1:
                        hidden_transpose(E_TILES - 1)
                        pe.wait_ge(sel_ready, it + 2)
                        bank_free(5, 3)
                        for i in range(3):
                            lo, n = UT[i]
                            mm = pe.transpose(bank[5][0:CAP, lo:lo + n], selw[0:n, i, :], ident[0:n, 0:n])
                        mm.then_inc(misc_done, 1)
                        for b in (1, 3):
                            bank_free(b, 3)
                        gather()
                    pe.wait_ge(low_done, it * E_CHUNKS + GU + j + 1)
                    t = j // 2
                    bank_free(4 + t % 2, t // 2 + 1)
                    for x in range(4):
                        f = 2 * j + x // 2
                        w = slice(x * WIDE, (x + 1) * WIDE)
                        mm = split_product(bank[6 + x % 2][0:CAP, :], hE_hi[:, f, :], hE_lo[:, f, :], high_slot(GU + j)[:, w],
                                           slot(GU + j, s5m_parts)[:, w], f == 0, f == F_EXP - 1)
                    mm.then_inc(mm_done, 1)
                for b in (6, 7):
                    bank_free(b, 1)
                bank_free(5, 4)
                for d in range(KD):
                    b = SCATTER[d % 4]
                    bank_free(b, SCATTER_USE[d % 4] + d // 4)
                    pe.matmul(bank[b][:, 0:T], ytok[0:CAP, d * P:(d + 1) * P], selT[0:CAP, :],
                              start=True, stop=True).then_inc(misc_done, 1)
            pe.wait_ge(squares, 7 * DEPTH + 1)
            pe.wait_ge(evicted[0], items * USES[0] + BASE[0])
            for k in range(KD):
                mm = pe.matmul(bank[0][:, 0:T], ones[:, :], uT[:, k, :], start=(k == 0), stop=(k == KD - 1))
            mm.then_inc(misc_done, 1)

        @block.scalar
        def _(act):
            order = [0]

            def link(ins):
                order[0] += 1
                ins.then_inc(act_order, 1)
                act.wait_ge(act_order, order[0])

            def full(key):
                act.wait_ge(mm_done, DONE[key])

            def copy_out(key, dst, src):
                full(key)
                act.activation(dst, src, ACT.Copy).then_inc(freed(key), 1)

            act.wait_ge(consts_in, 16 * 11)
            act.wait_ge(ones_set, 2)
            W = lambda i: lw[:, i, :]
            act.activation(W(0), lam[:, 2, :], ACT.Exp).then_inc(lam_act, 1)
            act.wait_ge(lam_ready, 1)
            act.activation(W(3), W(1), ACT.Exp).then_inc(lam_act, 1)
            act.activation(W(6), W(4), ACT.Sin).then_inc(lam_act, 1)
            act.activation(W(7), W(5), ACT.Sin).then_inc(lam_act, 1)

            def root(key, scale):
                full(key)
                act.activation(at(key)[:, 0:T], at(key)[:, 0:T], ACT.Sqrt, bias=eps[:, 0:1], scale=scale).then_inc(std_done, 1)

            for l in range(DEPTH):
                if l > 0:
                    act.wait_ge(*out_of((l - 1, "dn", 7)))
                    act.wait_ge(*out_of((l - 1, "dn", 6)))
                act.activation(uT[:, :, :], xT[:, :, :], ACT.Square).then_inc(squares, 1)
                root((l, "ms1", 0), 1.0 / D)
                for m in range(4):
                    full((l, "cb", m))
                    act.activation(sigb[:, m, :], at((l, "cb", m))[:, 0:T], ACT.Sigmoid, bias=vec(l, V_PWB, 4 + m)
                                   ).then_inc(freed((l, "cb", m)), 1)
                for m in range(4):
                    act.wait_ge(*out_of((l, "ca", m)))
                for m in range(4):
                    key = (l, "zs", m)
                    full(key)
                    act.activation(sigb[:, m, 0:SEQ].rearrange("p (s c) -> p s c", s=S),
                                   at(key)[:, 0:SEQ].rearrange("p (c s) -> p s c", s=S), ACT.Copy)
                    act.activation(sigb[:, m, SEQ:T], at(key)[:, SEQ:T], ACT.Copy).then_inc(freed(key), 1)
                for m in range(4):
                    act.wait_ge(*out_of((l, "zs", m)))
                act.dma_start(zscr.rearrange("(m p) t -> p m t", p=P), sigb[:, :, :]).then_inc(zscr_out, 16)
                for m in range(KD):
                    copy_out((l, "v", m), vT[:, m, :], at((l, "v", m))[:, 0:T])
                    if m == 2:
                        act.wait_ge(xin_zero, 1)
                        act.wait_ge(zscr_out, 16 * (l + 1))
                        zg = zscr.rearrange("(g p) t -> p g t", p=GP)
                        for s in range(S):
                            act.dma_start(xin[s * GP:(s + 1) * GP, :, 0:NC], zg[:, :, s * NC:(s + 1) * NC]).then_inc(xin_in, 16)
                        act.dma_start(xin[0:GP, :, NC:NC + NS], zg[:, :, SEQ:T]).then_inc(xin_in, 16)
                        act.dma_start(xin[P - GP:P, :, NC + NS:NC + 2 * NS], zg[:, :, SEQ:T]).then_inc(xin_in, 16)
                act.wait_ge(gb_ready, l + 1)
                for i in range(4):
                    copy_out((l, "vt", i), vtok[:, i // 2, (i % 2) * 512:(i % 2 + 1) * 512], at((l, "vt", i))[:, :])
                for i in range(2):
                    copy_out((l, "vs", i), vst[0:NS, i * 512:(i + 1) * 512], at((l, "vs", i))[0:NS, :])
                copy_out((l, "ks", 0), kst[0:NS, :], at((l, "ks", 0))[0:NS, :])
                for i in range(8):
                    copy_out((l, "win", i), winT[:, i * 512:(i + 1) * 512], at((l, "win", i))[:, :])
                for i in range(8):
                    copy_out((l, "kk", i), s5m[0:GP, i * 512:(i + 1) * 512], at((l, "kk", i))[0:GP, :])
                for h in range(HEADS):
                    key = (l, "ou", h)
                    full(key)
                    act.activation(vT[:, 2 * h:2 * h + 2, 0:SEQ], at(key)[:, :].rearrange("p (x t) -> p x t", x=2),
                                   ACT.Copy).then_inc(freed(key), 1)
                    key = (l, "st", h)
                    if l > 0 and h == 0:
                        act.wait_ge(st_out, 16 * l)
                    copy_out(key, stst[:, h, :], at(key)[:, 0:DV])
                for i in range(4):
                    key = (l, "si", i)
                    copy_out(key, si[:, :, 4 * i:4 * i + 4, :].rearrange("p r j c -> p j r c"),
                             at(key)[:, 0:384].rearrange("p (j r c) -> p j r c", j=4, r=2))
                act.wait_ge(*out_of((l, "cm", 0)))
                act.activation(sq[:, :].rearrange("p (m t) -> p m t", m=4), cT[:, :, :], ACT.Square).then_inc(squares, 1)
                root((l, "cv", 0), 1.0 / 512)
                act.wait_ge(cn_ready, l + 1)
                for m in range(4):
                    last = act.activation(cT[:, m, :], cT[:, m, :], ACT.Silu, bias=vec(l, V_LNB, m), scale=vec(l, V_LNG, m))
                last.then_inc(conv_act, 1)

                for d in range(KD):
                    key = (l, "gc", d)
                    full(key)
                    if d >= 2:
                        act.wait_ge(*out_of((l, "pc", d - 2)))
                    act.activation(gate[:, d % 2, :], at(key)[:, 0:T], ACT.Sigmoid).then_inc(freed(key), 1)
                    copy_out((l, "os", d), vT[:, :, SEQ + d:SEQ + d + 1], at((l, "os", d))[:, 0:KD].rearrange("p (m o) -> p m o", o=1))
                for h in range(HEADS):
                    act.wait_ge(*out_of((l, "gm", h)))
                    if h >= 2:
                        full((l, "gv", h - 2))
                    c = (h % 2) * 2 * T
                    act.activation(sq[:, c:c + 2 * T].rearrange("p (x t) -> p x t", x=2), vT[:, 2 * h:2 * h + 2, :],
                                   ACT.Square).then_inc(squares, 1)
                    if h >= 1:
                        root((l, "gv", h - 1), 1.0 / DV)
                root((l, "gv", 3), 1.0 / DV)
                for i in range(4):
                    copy_out((l, "y", i), ys[:, 8 * i:8 * i + 8, :], at((l, "y", i))[:, 0:320].rearrange("p (g c) -> p g c", g=8))
                for i in range(4):
                    act.wait_ge(*out_of((l, "y", i)))
                yd = yscr.rearrange("(g p) t -> p g t", p=GP)
                for s in range(S):
                    act.dma_start(yd[:, :, s * NC:(s + 1) * NC], ys[s * GP:(s + 1) * GP, :, 0:NC]).then_inc(yscr_out, 16)
                act.dma_start(yd[:, :, SEQ:T], ys[0:GP, :, NC:NC + NS]).then_inc(yscr_out, 16)
                for m in range(KD):
                    key = (l, "gg", m)
                    full(key)
                    if m >= 2:
                        act.wait_ge(gated, KD * l + m - 1)
                    else:
                        act.wait_ge(*out_of((l, "pc", 6 + m)))
                    act.activation(gate[:, m % 2, :], at(key)[:, 0:T], ACT.Silu).then_inc(freed(key), 1)
                act.wait_ge(yscr_out, 144 * (l + 1))
                act.dma_start(sigb[:, :, :], yscr.rearrange("(m p) t -> p m t", p=P)).then_inc(y_in, 16)
                for d in range(KD):
                    key = (l, "gr", d)
                    full(key)
                    if d >= 2:
                        act.wait_ge(*out_of((l, "pr", d - 2)))
                    else:
                        act.wait_ge(gated, KD * l + 7 + d)
                    act.activation(gate[:, d % 2, :], at(key)[:, 0:T], ACT.Sigmoid).then_inc(freed(key), 1)
                    if d == 1:
                        act.wait_ge(y_in, 16 * (l + 1))
                        act.wait_ge(conv_state_out, 32 * (l + 1))
                        act.activation(yg[:, :, 0:SEQ].rearrange("p m (c s) -> p m c s", s=S),
                                       sigb[:, :, 0:SEQ].rearrange("p m (s c) -> p m c s", s=S), ACT.Gelu_apprx_tanh)
                        act.activation(yg[:, :, SEQ:T], sigb[:, :, SEQ:T], ACT.Gelu_apprx_tanh).then_inc(gelu_done, 1)
                for m in range(4):
                    key = (l, "gl", m)
                    full(key)
                    if m >= 2:
                        act.wait_ge(glu_done, 4 * l + m - 1)
                    else:
                        act.wait_ge(*out_of((l, "pr", 6 + m)))
                    act.activation(gate[:, m % 2, :], at(key)[:, 0:T], ACT.Sigmoid, bias=vec(l, V_GLB, m)).then_inc(freed(key), 1)
                for d in range(KD):
                    key = (l, "gs", d)
                    full(key)
                    if d >= 2:
                        act.wait_ge(*out_of((l, "ps", d - 2)))
                    else:
                        act.wait_ge(glu_done, 4 * l + 3 + d)
                    act.activation(gate[:, d % 2, :], at(key)[:, 0:T], ACT.Sigmoid).then_inc(freed(key), 1)
                for d in range(KD):
                    act.wait_ge(*out_of((l, "wo", d)))
                act.activation(uT[:, :, :], xT[:, :, :], ACT.Square).then_inc(squares, 1)
                root((l, "ms2", 0), 1.0 / D)
                if l == 0:
                    for f in range(F_DENSE):
                        key = (l, "fg", f)
                        full(key)
                        if f >= 2:
                            act.wait_ge(*out_of((l, "fu", f - 2)))
                        else:
                            act.wait_ge(*out_of((l, "ps", 6 + f)))
                        act.activation(gate[:, f % 2, :], at(key)[:, 0:T], ACT.Silu).then_inc(freed(key), 1)

            l = DEPTH - 1
            act.wait_ge(s_out[0], 64 * DEPTH)
            act.wait_ge(s_out[1], 64 * DEPTH)
            act.wait_ge(st_out, 16 * DEPTH)
            for i in range(6):
                n = UT[i // 2][1]
                copy_out((l, "tt", i), utok[0:n, i // 2, (i % 2) * 512:(i % 2 + 1) * 512], at((l, "tt", i))[0:n, :])
            act.wait_ge(route_act, 1)
            act.activation(rt[:, 2, :, 0:1], rt[:, 1, :, 0:1], ACT.Exp).then_inc(route_act, 1)
            act.wait_ge(items_ready, 1)
            items = act.value_load(items_t[0:1, 0:1], min_val=NEXP, max_val=3 * NEXP)

            def gathered(turn):
                for half in range(2):
                    act.wait_ge(misc_done, turn + half)
                    act.activation(xg_hi[:, 4 * half:4 * half + 4, :],
                                   bank[1 + 2 * half][:, 0:4 * CAP].rearrange("p (k c) -> p k c", k=4), ACT.Copy
                                   ).then_inc(gathered_high, 1)

            gathered(1)
            with act.Fori(0, items) as it:

                def high(c):
                    act.wait_ge(mloaded[c % MRING], (it * TURNS + c // MRING + 1) * 16)
                    act.wait_ge(mm_done, it * E_CHUNKS + MM_BASE + c - HRING + 1)
                    act.activation(high_slot(c), slot(c, s5m), ACT.Copy).then_inc(high_done, 1)

                for c in range(AHEAD):
                    high(c)
                for c in range(E_CHUNKS):
                    t = c // 4
                    if c < GU and c % 4 == 1:
                        act.wait_ge(mm_done, it * E_CHUNKS + MM_BASE + c + 1)
                        act.activation(hm[0:CAP, t % 2, :], bank[t % 2][0:CAP, :], ACT.Silu).then_inc(evicted[t % 2], 1)
                    if c == GU + 1 or (c < GU and c % 4 == 2 and c > 4):
                        act.wait_ge(misc_done, it * MISC + MISC0 + t)
                        act.activation(hE_hi[:, 4 * t - 4:4 * t, :],
                                       bank[4 + (t - 1) % 2][:, 0:4 * CAP].rearrange("p (k c) -> p k c", k=4), ACT.Copy
                                       ).then_inc(hidden_high, 1)
                    if c == GU + 1:
                        act.wait_ge(misc_done, it * MISC + MISC0 + M_ONEHOT + 1)
                        act.activation(selT[0:CAP, :], bank[5][0:CAP, 0:T], ACT.Copy).then_inc(evicted[5], 1)
                        gathered(it * MISC + MISC0 + M_GATHER + 1)
                    if c + AHEAD < E_CHUNKS:
                        high(c + AHEAD)
                act.wait_ge(mm_done, it * E_CHUNKS + MM_BASE + E_CHUNKS)
                act.activation(ytok[0:CAP, 0:WIDE], bank[6][0:CAP, :], ACT.Copy).then_inc(evicted[6], 1)
            for b in SCATTER:
                act.wait_ge(evicted[b], items * USES[b] + BASE[b])
            act.activation(uT[:, :, :], xT[:, :, :], ACT.Square).then_inc(squares, 1)
            act.wait_ge(misc_done, items * MISC + MISC0 + 1)
            act.activation(bank[0][:, 0:T], bank[0][:, 0:T], ACT.Sqrt, bias=eps[:, 0:1], scale=1.0 / D).then_inc(std_done, 1)

        @block.vector
        def _(dve):
            order = [0]

            def link(ins):
                order[0] += 1
                ins.then_inc(dve_order, 1)
                dve.wait_ge(dve_order, order[0])

            def full(key):
                dve.wait_ge(mm_done, DONE[key])

            def mul(out, x, y):
                return dve.tensor_tensor(out, x, y, ALU.mult)

            def add(out, x, y):
                return dve.tensor_tensor(out, x, y, ALU.add)

            dve.memset(ones[:, :], 1.0).then_inc(ones_set, 1)
            dve.memset(eps[:, :], EPS).then_inc(ones_set, 1)
            dve.wait_ge(consts_in, 16 * 11)
            W = lambda i: lw[:, i, :]
            lre, lim = lam[:, 0, :], lam[:, 1, :]
            TWO_PI_HI = 6.28125
            TWO_PI_LO = 2 * np.pi - 6.28125
            ROUND = 1.5 * 2 ** 23
            HALF_PI = np.pi / 2
            PI_DOWN = 3.1415925
            dve.wait_ge(lam_act, 1)
            link(mul(W(1), lre, W(0)))
            link(mul(W(2), lim, W(0)))
            link(dve.tensor_scalar(W(14), W(2), 1 / (2 * np.pi), None, ALU.mult))
            link(dve.tensor_scalar(W(14), W(14), ROUND, None, ALU.add))
            link(dve.tensor_scalar(W(14), W(14), -ROUND, None, ALU.add))
            link(dve.scalar_tensor_tensor(out=W(4), in0=W(14), scalar=-TWO_PI_HI, in1=W(2), op0=ALU.mult, op1=ALU.add))
            link(dve.scalar_tensor_tensor(out=W(4), in0=W(14), scalar=-TWO_PI_LO, in1=W(4), op0=ALU.mult, op1=ALU.add))
            link(dve.tensor_scalar(W(4), W(4), PI_DOWN, -PI_DOWN, ALU.min, ALU.max))
            link(dve.tensor_scalar(W(15), W(4), -1.0, None, ALU.mult))
            link(dve.tensor_tensor(W(15), W(15), W(4), ALU.max))
            dve.tensor_scalar(W(5), W(15), -1.0, HALF_PI, ALU.mult, ALU.add).then_inc(lam_ready, 1)
            link(mul(W(10), lre, lre))
            link(mul(W(14), lim, lim))
            link(add(W(10), W(10), W(14)))
            link(dve.reciprocal(W(10), W(10)))
            dve.wait_ge(lam_act, 4)
            link(mul(W(8), W(3), W(7)))
            link(mul(W(9), W(3), W(6)))
            link(dve.tensor_scalar(W(11), W(8), -1.0, None, ALU.add))
            link(mul(W(12), W(11), lre))
            link(mul(W(14), W(9), lim))
            link(add(W(12), W(12), W(14)))
            link(mul(W(12), W(12), W(10)))
            link(mul(W(13), W(9), lre))
            link(mul(W(14), W(11), lim))
            link(dve.tensor_tensor(W(13), W(13), W(14), ALU.subtract))
            mul(W(13), W(13), W(10)).then_inc(lam_ready, 1)

            def normed(key, gains, turn, signal):
                dve.wait_ge(std_done, turn)
                dve.reciprocal(rstd[:, 0, :], at(key)[:, 0:T]).then_inc(freed(key), 1)
                dve.wait_ge(*out_of(key))
                for d in range(KD):
                    last = dve.scalar_tensor_tensor(out=uT[:, d, :], in0=xT[:, d, :], scalar=gains(d), in1=rstd[:, 0, :],
                                                    op0=ALU.mult, op1=ALU.mult)
                last.then_inc(signal, 1)

            def conv_ops(l, lo, hi):
                for n in range(lo, hi):
                    k, m = n // 4, n % 4
                    if k == 0:
                        dve.wait_ge(*out_of((l, "ca", m)))
                        dve.tensor_scalar(cT[:, m, 0:SEQ], xc[:, m, 0:SEQ], vec(l, V_DWW, m * TAPS), vec(l, V_DWB, m),
                                          ALU.mult, ALU.add).then_inc(conv_step, 1)
                    else:
                        dve.wait_ge(conv_step, l * 4 * TAPS + n - 3)
                        dve.scalar_tensor_tensor(out=cT[:, m, 0:SEQ], in0=xc[:, m, k:k + SEQ],
                                                 scalar=vec(l, V_DWW, m * TAPS + k), in1=cT[:, m, 0:SEQ],
                                                 op0=ALU.mult, op1=ALU.add).then_inc(conv_step, 1)

            def recur(l, lo, hi):
                for c in range(lo, hi):
                    to = c + 1 if c + 1 < NC else NC + NS
                    now = hst[:, :, :, c]
                    mul(rec[:, 0, :, :], now, l8[:, 0:2, :]).then_inc(dve_order, 1)
                    mul(rec[:, 1, 0, :], hst[:, 1, :, c], l8[:, 2, :]).then_inc(dve_order, 1)
                    mul(rec[:, 1, 1, :], hst[:, 0, :, c], l8[:, 3, :]).then_inc(dve_order, 1)
                    order[0] += 3
                    dve.wait_ge(dve_order, order[0] - 2)
                    link(add(rec[:, 2, :, :], rec[:, 0, :, :], si[:, :, :, c]))
                    link(add(hst[:, :, :, to], rec[:, 1, :, :], rec[:, 2, :, :]))

            for l in range(DEPTH):
                normed((l, "ms1", 0), lambda d: vec(l, V_GM, d), 7 * l + 1, u_ready)
                link(dve.memset(xc[:, :, 0:TAPS - 1], 0.0))
                for m in range(4):
                    key = (l, "ca", m)
                    dve.wait_ge(*out_of((l, "cb", m)))
                    full(key)
                    dve.scalar_tensor_tensor(out=xc[:, m, TAPS - 1:TAPS - 1 + SEQ], in0=at(key)[:, 0:SEQ],
                                             scalar=vec(l, V_PWB, m), in1=sigb[:, m, 0:SEQ], op0=ALU.add, op1=ALU.mult)
                    dve.scalar_tensor_tensor(out=xs[:, m, :, TAPS - 1], in0=at(key)[:, SEQ:T],
                                             scalar=vec(l, V_PWB, m), in1=sigb[:, m, SEQ:T], op0=ALU.add, op1=ALU.mult
                                             ).then_inc(freed(key), 1)
                conv_ops(l, 0, 28)
                for n in range(8):
                    name, h = ("q", n) if n < 4 else ("k", n - 4)
                    to = qT if n < 4 else kT
                    w = 0 if n < 4 else 2
                    key = (l, name, h)
                    full(key)
                    if n > 0:
                        prev = (l, "q", n - 1) if n <= 4 else (l, "k", n - 5)
                        dve.wait_ge(*out_of(prev))
                    mul(tmp[:, 0, :], at(key)[:, 0:T], rope[:, w, :])
                    mul(tmp[0:64, 1, :], at(key)[64:P, 0:T], rope[64:P, w + 1, :])
                    link(mul(tmp[64:P, 1, :], at(key)[0:64, 0:T], rope[0:64, w + 1, :]))
                    add(to[:, h, :], tmp[:, 0, :], tmp[:, 1, :]).then_inc(freed(key), 1)
                    conv_ops(l, 28 + 6 * n, 34 + 6 * n)
                dve.wait_ge(*out_of((l, "q", 3)))
                dve.tensor_copy(qs[:, :, :], qT[:, :, SEQ:T]).then_inc(qs_ready, 1)
                conv_ops(l, 76, 4 * TAPS)
                dve.wait_ge(conv_state_in, 16 * (l + 1))
                dve.wait_ge(*out_of((l, "k", 3)))
                prod = tmp[:, :, :].rearrange("p a t -> p (a t)")[:, 0:NS * TAPS].rearrange("p (b k) -> p b k", b=NS)
                for m in range(4):
                    taps = vecs[:, l * V_L + V_DWW + m * TAPS:l * V_L + V_DWW + (m + 1) * TAPS]
                    link(mul(prod, xs[:, m, :, :], taps.unsqueeze(1).broadcast_to([P, NS, TAPS])))
                    link(dve.tensor_reduce(cT[:, m, SEQ:T], prod, AX, ALU.add))
                    if m < 3:
                        link(dve.tensor_scalar(cT[:, m, SEQ:T], cT[:, m, SEQ:T], vec(l, V_DWB, m), None, ALU.add))
                dve.wait_ge(conv_step, (l + 1) * 4 * TAPS)
                dve.tensor_scalar(cT[:, 3, SEQ:T], cT[:, 3, SEQ:T], vec(l, V_DWB, 3), None, ALU.add).then_inc(conv_done, 1)
                dve.wait_ge(gb_ready, l + 1)
                for i in range(2):
                    key = (l, "kt", i)
                    full(key)
                    dve.tensor_tensor(kd[:, i, :].rearrange("p (h x) -> p h x", h=HEADS),
                                      at(key)[:, :].rearrange("p (h x) -> p h x", h=HEADS),
                                      kdec[:, i, :].unsqueeze(2).broadcast_to([P, HEADS, P]), ALU.mult).then_inc(freed(key), 1)
                for h in range(HEADS):
                    key = (l, "sc", h)
                    full(key)
                    mul(pt[:, h % 2, 0:SEQ], at(key)[:, 0:SEQ], decay[:, h, :])
                    mul(pt[:, h % 2, SEQ:SEQ + P], at(key)[:, SEQ:SEQ + P], decay[:, h, 0:P]).then_inc(freed(key), 1)
                key = (l, "cm", 0)
                full(key)
                dve.scalar_tensor_tensor(out=cT[:, :, :], in0=at(key)[:, 0:T].unsqueeze(1).broadcast_to([P, 4, T]),
                                         scalar=-1.0 / 512, in1=cT[:, :, :], op0=ALU.mult, op1=ALU.add).then_inc(freed(key), 1)

                def kmasked(b):
                    if b >= 2:
                        full((l, "ob", b - 2))
                    dve.tensor_scalar(kmask[0:NS, b % 2, :], kst[0:NS, :], ident[0:NS, b:b + 1], None, ALU.mult
                                      ).then_inc(kmask_ready, 1)

                dve.wait_ge(*out_of((l, "ks", 0)))
                kmasked(0)
                kmasked(1)
                key = (l, "cv", 0)
                dve.wait_ge(std_done, 7 * l + 2)
                dve.reciprocal(rstd[:, 0, :], at(key)[:, 0:T]).then_inc(freed(key), 1)
                dve.wait_ge(*out_of(key))
                mul(cT[:, :, :], cT[:, :, :], rstd[:, 0, :].unsqueeze(1).broadcast_to([P, 4, T])).then_inc(cn_ready, 1)
                for i in range(4):
                    dve.wait_ge(*out_of((l, "si", i)))
                dve.wait_ge(l8_ready, l + 1)
                dve.wait_ge(h0_in, 16 * (l + 1))
                link(dve.memset(hst[:, :, :, 0:1], 0.0))
                for d in range(KD):
                    recur(l, 4 * d, 4 * d + 4)
                    key = (l, "pc", d)
                    dve.wait_ge(*out_of((l, "gc", d)))
                    full(key)
                    mul(mT[:, d, :], at(key)[:, 0:T], gate[:, d % 2, :]).then_inc(freed(key), 1)
                    dve.wait_ge(s_in[d % 2], 16 * (4 * l + d // 2 + 1))
                    for half, name in ((0, "oa"), (1, "ob")):
                        key = (l, name, d)
                        full(key)
                        for x in range(2):
                            h = 2 * half + x
                            s = sring[:, d % 2, h, :]
                            last = dve.scalar_tensor_tensor(out=s, in0=s, scalar=1.0 - 2.0 ** (-5 - h),
                                                            in1=at(key)[:, x * DV:(x + 1) * DV], op0=ALU.mult, op1=ALU.add)
                        last.then_inc(freed(key), 1)
                    if d + 2 < NS:
                        kmasked(d + 2)
                if l > 0:
                    dve.wait_ge(hstate_out, 32 * l)
                link(dve.tensor_copy(hfin[:, :, :], hst[:, :, :, NC + NS]))
                h0 = hst[:, :, :, NC:NC + NS]
                lb = [lw[:, w, l * GJ:(l + 1) * GJ] for w in (8, 9)]
                t = tmp[:, 0, 0:GJ * NS].rearrange("p (j b) -> p j b", j=GJ)
                wide = [P, GJ, NS]
                for ri in range(2):
                    link(mul(hnew[:, ri, :, :], h0[:, ri, :, :], lb[0].unsqueeze(2).broadcast_to(wide)))
                    link(mul(t, h0[:, 1 - ri, :, :], lb[1].unsqueeze(2).broadcast_to(wide)))
                    link(dve.tensor_tensor(hnew[:, ri, :, :], hnew[:, ri, :, :], t, ALU.add if ri else ALU.subtract))
                add(hnew[:, :, :, :], hnew[:, :, :, :], si[:, :, :, NC + NS:NC + 2 * NS]).then_inc(h_ready, 1)
                for h in range(HEADS):
                    key = (l, "gm", h)
                    full(key)
                    dve.scalar_tensor_tensor(out=vT[:, 2 * h:2 * h + 2, :],
                                             in0=at(key)[:, 0:T].unsqueeze(1).broadcast_to([P, 2, T]), scalar=-1.0 / DV,
                                             in1=vT[:, 2 * h:2 * h + 2, :], op0=ALU.mult, op1=ALU.add).then_inc(freed(key), 1)
                for h in range(HEADS):
                    key = (l, "gv", h)
                    dve.wait_ge(std_done, 7 * l + 3 + h)
                    dve.reciprocal(rstd[:, h % 2, :], at(key)[:, 0:T]).then_inc(freed(key), 1)
                    dve.wait_ge(*out_of(key))
                    link(mul(vT[:, 2 * h:2 * h + 2, :], vT[:, 2 * h:2 * h + 2, :],
                             rstd[:, h % 2, :].unsqueeze(1).broadcast_to([P, 2, T])))
                for m in range(KD):
                    dve.wait_ge(*out_of((l, "gg", m)))
                    mul(vT[:, m, :], vT[:, m, :], gate[:, m % 2, :]).then_inc(gated, 1)

                def merge(gate_name, proj_name, turn):
                    for d in range(KD):
                        key = (l, proj_name, d)
                        dve.wait_ge(*out_of((l, gate_name, d)))
                        full(key)
                        mul(tmp[:, d % 2, :], at(key)[:, 0:T], gate[:, d % 2, :]).then_inc(freed(key), 1)
                        dve.wait_ge(*out_of(key))
                        if turn == 0:
                            dve.wait_ge(*out_of((l, "pc", d)))
                        else:
                            dve.wait_ge(merged, 16 * l + d + 1)
                        add(mT[:, d, :], mT[:, d, :], tmp[:, d % 2, :]).then_inc(merged, 1)

                merge("gr", "pr", 0)
                for m in range(4):
                    dve.wait_ge(*out_of((l, "gl", m)))
                    mul(sigb[:, m, :], yg[:, m, :], gate[:, m % 2, :]).then_inc(glu_done, 1)
                merge("gs", "ps", 1)
                for d in range(KD):
                    key = (l, "wo", d)
                    full(key)
                    add(xT[:, d, :], xT[:, d, :], at(key)[:, 0:T]).then_inc(freed(key), 1)
                normed((l, "ms2", 0), lambda d: vec(l, V_GF, d), 7 * l + 7, u_ready)
                if l == 0:
                    for f in range(F_DENSE):
                        key = (l, "fu", f)
                        dve.wait_ge(*out_of((l, "fg", f)))
                        full(key)
                        mul(hT[:, f, :], at(key)[:, 0:T], gate[:, f % 2, :]).then_inc(freed(key), 1)
                    for d in range(KD):
                        key = (l, "dn", d)
                        full(key)
                        add(xT[:, d, :], xT[:, d, :], at(key)[:, 0:T]).then_inc(freed(key), 1)

            l = DEPTH - 1
            R = lambda w: rt[:, w, :, :]
            R1 = lambda w, c=0: rt[:, w, :, c:c + 1]
            for b in range(2):
                dve.wait_ge(s_out[b], 64 * DEPTH)
            dve.wait_ge(st_out, 16 * DEPTH)
            dve.wait_ge(hstate_out, 32 * DEPTH)
            link(dve.memset(rt[:, :, :, :], 0.0))
            link(dve.memset(slotx[:, :, :], -BIG))
            link(dve.memset(combx[:, :, :], 0.0))
            for i in range(3):
                key = (l, "lg", i)
                full(key)
                n = UT[i][1]
                dve.tensor_copy(rt[0:n, 0, i, :], at(key)[0:n, 0:NEXP]).then_inc(freed(key), 1)
            for i in range(3):
                dve.wait_ge(*out_of((l, "lg", i)))
                link(dve.max(rt[:, 8, i, :], rt[:, 0, i, :]))
                link(dve.max_index(rti[:, i, :], rt[:, 8, i, :], rt[:, 0, i, :]))
            link(dve.tensor_copy(R(9), rti[:, :, :]))
            wide = [P, 3, NEXP]
            eight = iota[:, 0:NEXP].unsqueeze(1).broadcast_to(wide)
            dve.tensor_tensor(R1(1), R1(8, 1), R1(8, 0), ALU.subtract).then_inc(route_act, 1)
            link(dve.tensor_tensor(R(10), eight, R1(9, 0).broadcast_to(wide), ALU.is_equal))
            link(dve.tensor_tensor(R(11), eight, R1(9, 1).broadcast_to(wide), ALU.is_equal))
            add(R(6), R(10), R(11)).then_inc(route_ready, 1)
            dve.wait_ge(route_act, 2)
            link(dve.tensor_scalar(R1(3), R1(2), 1.0, None, ALU.add))
            link(dve.reciprocal(R1(4), R1(3)))
            link(mul(R1(5), R1(2), R1(4)))
            link(mul(R(13), R(10), R1(4).broadcast_to(wide)))
            link(mul(R(14), R(11), R1(5).broadcast_to(wide)))
            link(add(R(7), R(13), R(14)))
            dve.wait_ge(route_ready, 1)
            link(dve.tensor_scalar(R(15), R(6), BIG, -BIG, ALU.mult, ALU.add))
            key = (l, "po", 0)
            full(key)
            o = at(key)
            link(add(rt[:, 12, 0:2, :], rt[:, 15, 0:2, :], o[:, 0:16].rearrange("p (i e) -> p i e", i=2)))
            link(add(rt[0:NS, 12, 2, :], rt[0:NS, 15, 2, :], o[0:NS, 16:24]))
            dve.tensor_reduce(rt[:, 16, 0, 0:1], o[:, 24:32], AX, ALU.max).then_inc(freed(key), 1)
            dve.wait_ge(*out_of(key))
            link(dve.tensor_scalar(rt[:, 16, 0, 1:2], rt[:, 16, 0, 0:1], float(CAP), None, ALU.is_gt))
            link(dve.tensor_scalar(rt[:, 16, 0, 2:3], rt[:, 16, 0, 0:1], float(2 * CAP), None, ALU.is_gt))
            link(add(rt[:, 16, 0, 3:4], rt[:, 16, 0, 1:2], rt[:, 16, 0, 2:3]))
            dve.tensor_scalar(items_t[:, :], rt[:, 16, 0, 3:4], float(NEXP), float(NEXP), ALU.mult, ALU.add
                              ).then_inc(items_ready, 1)
            for r in range(3):
                c = slice(r * NEXP, (r + 1) * NEXP)
                link(dve.tensor_scalar(slotx[:, :, c], R(12), -float(CAP * r), None, ALU.add))
                link(dve.tensor_copy(combx[:, :, c], R(7)))
            for i in range(3):
                last = dve.tensor_scalar(sel[:, i, :], iota[:, :], slotx[:, i, 0:1], None, ALU.is_equal)
            last.then_inc(sel_ready, 1)
            dve.wait_ge(items_ready, 1)
            items = dve.value_load(items_t[0:1, 0:1], min_val=NEXP, max_val=3 * NEXP)
            def gathered(turn):
                for half in range(2):
                    dve.wait_ge(gathered_high, turn + half)
                    x = xg_hi[:, 4 * half:4 * half + 4, :]
                    dve.tensor_tensor(xg_lo[:, 4 * half:4 * half + 4, :],
                                      bank[1 + 2 * half][:, 0:4 * CAP].rearrange("p (k c) -> p k c", k=4), f32(x), ALU.subtract
                                      ).then_inc(evicted[1 + 2 * half], 1)

            gathered(1)
            with dve.Fori(0, items) as it:

                def low(c):
                    dve.wait_ge(high_done, it * E_CHUNKS + c + 1)
                    dve.tensor_tensor(slot(c, s5m_parts), slot(c, s5m), f32(high_slot(c)), ALU.subtract).then_inc(low_done, 1)

                for c in range(AHEAD):
                    low(c)
                for c in range(E_CHUNKS):
                    t = c // 4
                    if c < GU and c % 4 == 3:
                        dve.wait_ge(mm_done, it * E_CHUNKS + MM_BASE + c + 1)
                        dve.wait_ge(evicted[t % 2], it * USES[t % 2] + BASE[t % 2] + t // 2 + 1)
                        mul(hm[0:CAP, t % 2, :], hm[0:CAP, t % 2, :], bank[2 + t % 2][0:CAP, :]).then_inc(evicted[2 + t % 2], 1)
                    if c == GU + 1 or (c < GU and c % 4 == 2 and c > 4):
                        b = 4 + (t - 1) % 2
                        dve.wait_ge(hidden_high, it * E_TILES + t)
                        dve.tensor_tensor(hE_lo[:, 4 * t - 4:4 * t, :], bank[b][:, 0:4 * CAP].rearrange("p (k c) -> p k c", k=4),
                                          f32(hE_hi[:, 4 * t - 4:4 * t, :]), ALU.subtract).then_inc(evicted[b], 1)
                    if c == GU + 1:
                        gathered(it * 2 + 3)
                    if c == 9:
                        dve.wait_ge(misc_done, it * MISC + MISC0)
                        dve.tensor_copy(cur[:, 0, :], slotx[:, :, bass.ds(it + 1, 1)].rearrange("p i o -> p (i o)")).then_inc(cur_ready, 1)
                        dve.tensor_copy(cur[:, 1, :], slotx[:, :, bass.ds(it, 1)].rearrange("p i o -> p (i o)")).then_inc(cur_ready, 1)
                        dve.tensor_copy(cur[:, 2, :], combx[:, :, bass.ds(it, 1)].rearrange("p i o -> p (i o)")).then_inc(cur_ready, 1)
                        dve.wait_ge(cur_ready, it * 3 + 3)
                        for i in range(3):
                            dve.tensor_scalar(sel[:, i, :], iota[:, :], cur[:, 0, i:i + 1], None, ALU.is_equal)
                            last = dve.tensor_scalar(selw[:, i, :], iota[:, :], cur[:, 1, i:i + 1], cur[:, 2, i:i + 1],
                                                     ALU.is_equal, ALU.mult)
                        last.then_inc(sel_ready, 1)
                    if c + AHEAD < E_CHUNKS:
                        low(c + AHEAD)
                dve.wait_ge(mm_done, it * E_CHUNKS + MM_BASE + E_CHUNKS)
                dve.tensor_copy(ytok[0:CAP, WIDE:D], bank[7][0:CAP, :]).then_inc(evicted[7], 1)
                for d in range(KD):
                    b = SCATTER[d % 4]
                    dve.wait_ge(misc_done, it * MISC + MISC0 + M_SCATTER + d + 1)
                    add(xT[:, d, :], xT[:, d, :], bank[b][:, 0:T]).then_inc(evicted[b], 1)
            dve.wait_ge(std_done, 7 * DEPTH + 1)
            link(dve.reciprocal(rstd[:, 0, :], bank[0][:, 0:T]))
            for d in range(KD):
                last = dve.scalar_tensor_tensor(out=uT[:, d, :], in0=xT[:, d, :], scalar=vecs[:, V_FIN + d:V_FIN + d + 1],
                                                in1=rstd[:, 0, :], op0=ALU.mult, op1=ALU.mult)
            last.then_inc(x_final, 1)

        @block.gpsimd
        def _(pool):
            order = [0]

            def link(ins):
                order[0] += 1
                ins.then_inc(pool_order, 1)
                pool.wait_ge(pool_order, order[0])

            def mul(out, x, y):
                return pool.tensor_tensor(out, x, y, ALU.mult)

            def product(out, x, y, t):
                link(mul(out[0], x[0], y[0]))
                link(mul(t, x[1], y[1]))
                link(pool.tensor_tensor(out[0], out[0], t, ALU.subtract))
                link(mul(out[1], x[0], y[1]))
                link(mul(t, x[1], y[0]))
                link(pool.tensor_tensor(out[1], out[1], t, ALU.add))

            link(pool.memset(s5m[0:GP, 0:G * P], 0.0))
            pool.dma_start(kscr.rearrange("g p x -> p g x")[:, :, 0:P],
                           s5m[0:GP, 0:G * P].rearrange("p (g x) -> p g x", g=G)).then_inc(zero_out, 16)
            pool.memset(xin[:, :, :], 0.0).then_inc(xin_zero, 1)
            pool.wait_ge(zero_out, 16)
            pool.wait_ge(consts_in, 16 * 11)
            pool.wait_ge(lam_ready, 2)
            for l in range(DEPTH):
                if l > 0:
                    pool.wait_ge(mm_done, DONE[(l - 1, "y", 3)])
                    pool.wait_ge(hstate_out, 32 * l)
                    for b in range(2):
                        pool.wait_ge(s_out[b], 64 * l)
                    pool.wait_ge(st_out, 16 * l)
                pool.dma_start(work[:, 0:1024], a["bc"][l]).then_inc(bc_in, 16)
                pool.dma_start(hst[:, :, :, NC:NC + NS], a["h0"][l]).then_inc(h0_in, 16)
                ls = slice(l * GJ, (l + 1) * GJ)
                link(pool.memset(pa[:, 0, 0, :], 1.0))
                link(pool.memset(pa[:, 1, 0, :], 0.0))
                link(pool.tensor_copy(pa[:, 0, 1, :], lw[:, 8, ls]))
                link(pool.tensor_copy(pa[:, 1, 1, :], lw[:, 9, ls]))

                def powers(lo, n, by):
                    x = [pa[:, r, lo:lo + n, :] for r in range(2)]
                    y = [pa[:, r, by:by + 1, :].broadcast_to([P, n, GJ]) for r in range(2)]
                    out = [pa[:, r, lo + by:lo + by + n, :] for r in range(2)]
                    product(out, x, y, pw[:, 0, 0:n, :])

                powers(1, 1, 1)
                powers(1, 2, 2)
                powers(1, 4, 4)
                for s in range(S):
                    link(pool.tensor_copy(pd[:, :, s, :], pa[:, :, S - 1 - s, :]))
                for w, r in ((0, 0), (1, 0), (3, 1)):
                    link(pool.tensor_copy(l8[:, w, :], pa[:, r, S, :]))
                pool.tensor_scalar(l8[:, 2, :], pa[:, 1, S, :], -1.0, 0.0, ALU.mult, ALU.add).then_inc(l8_ready, 1)
                pool.wait_ge(bc_in, 16 * (l + 1))
                flat = [P, GJ, GP]
                f = [lw[:, w, ls].unsqueeze(2).broadcast_to(flat) for w in (12, 13)]
                t = pt1[:, 0:GJ * GP].rearrange("p (j q) -> p j q", j=GJ)
                product([bb[:, r] for r in range(2)], f, [bc[:, r] for r in range(2)], t)
                wide = [P, GJ, S, GP]
                x = [pd[:, r].rearrange("p s j -> p j s").unsqueeze(3).broadcast_to(wide) for r in range(2)]
                y = [bb[:, r].unsqueeze(2).broadcast_to(wide) for r in range(2)]
                t = pt1[:, 0:GJ * S * GP].rearrange("p (j s q) -> p j s q", j=GJ, s=S)
                product([gb[:, :, r] for r in range(2)], x, y, t)
                wide = [P, GJ, S + 1, GP]
                x = [pa[:, r].rearrange("p k j -> p j k").unsqueeze(3).broadcast_to(wide) for r in range(2)]
                y = [bc[:, 2 + r].unsqueeze(2).broadcast_to(wide) for r in range(2)]
                t = pt1[:, 0:GJ * 9 * GP].rearrange("p (j s q) -> p j s q", j=GJ, s=9)
                product([v.rearrange("p j (k q) -> p j k q", q=GP) for v in (clr, cli)], x, y, t)
                link(pool.tensor_scalar(cli[:, :, :], cli[:, :, :], -1.0, 0.0, ALU.mult, ALU.add))
                few = [GP, G, GP]
                mul(dd, ident[0:GP, 0:GP].unsqueeze(1).broadcast_to(few), dskip[:, l, :].unsqueeze(2).broadcast_to(few)
                    ).then_inc(gb_ready, 1)
                if l > 0:
                    pool.wait_ge(mm_done, DONE[(l - 1, "dn", 7)])
                pool.dma_start(xs[:, :, :, 0:TAPS - 1], a["convst"][l]).then_inc(conv_state_in, 16)
                for i in range(8):
                    pool.wait_ge(*out_of((l, "kk", i)))
                pool.wait_ge(gb_ready, l + 1)
                pool.tensor_tensor(toep[0:GP, :, 0:GP], toep[0:GP, :, 0:GP], dd, ALU.add).then_inc(kmat_ready, 1)
                pool.wait_ge(kmat_ready, l + 1)
                pool.dma_start(kscr.rearrange("g p x -> p g x")[:, :, P:2 * P], toep[0:GP, :, :]).then_inc(kscr_out, 16)
                for b in range(2):
                    pool.dma_start(sring[:, b, :, :], a["sret"][l, b].rearrange("h d v -> d h v")).then_inc(s_in[b], 16)
                pool.wait_ge(kscr_out, 16 * (l + 1))
                for s in range(S):
                    pool.dma_start(toep[s * GP:(s + 1) * GP, :, :],
                                   kscr.rearrange("g p x -> p g x")[:, :, P - GP * s:2 * P - GP * s]).then_inc(toep_in, 16)
                for m in range(4):
                    pool.wait_ge(*out_of((l, "ca", m)))
                pool.wait_ge(conv_state_in, 16 * (l + 1))
                pool.dma_start(a["conv_p"][l], xc[:, :, SEQ:SEQ + TAPS - 1]).then_inc(conv_state_out, 16)
                pool.dma_start(a["conv_s"][l], xs[:, :, :, 1:TAPS]).then_inc(conv_state_out, 16)
                for h in range(HEADS):
                    pool.wait_ge(*out_of((l, "st", h)))
                pool.dma_start(a["ret_p"][l].rearrange("h d v -> d h v"), stst[:, :, :]).then_inc(st_out, 16)
                for b in range(NS):
                    pool.wait_ge(*out_of((l, "oa", b)))
                    pool.wait_ge(*out_of((l, "ob", b)))
                    pool.dma_start(a["ret_s"][l, b].rearrange("h d v -> d h v"), sring[:, b % 2, :, :]).then_inc(s_out[b % 2], 16)
                    if b + 2 < NS:
                        pool.wait_ge(mm_done, DONE[(l, "os", b)])
                        pool.wait_ge(s_out[b % 2], 16 * (4 * l + b // 2 + 1))
                        pool.dma_start(sring[:, b % 2, :, :], a["sret"][l, b + 2].rearrange("h d v -> d h v")).then_inc(s_in[b % 2], 16)
                pool.wait_ge(h_ready, l + 1)
                pool.dma_start(a["h_p"][l], hfin[:, :, :]).then_inc(hstate_out, 16)
                pool.dma_start(a["h_s"][l], hnew[:, :, :, :]).then_inc(hstate_out, 16)
            pool.wait_ge(hstate_out, 32 * DEPTH)
            pool.wait_ge(conv_state_out, 32 * DEPTH)
            pool.wait_ge(st_out, 16 * DEPTH)
            for b in range(2):
                pool.wait_ge(s_out[b], 64 * DEPTH)


def _blocks(w):
    k, m = w.shape
    return w.reshape(k // P, P, m // P, P).transpose(2, 0, 1, 3)


def _stream(parts):
    b = np.concatenate([p.reshape(-1, P, P) for p in parts])
    return b.reshape(-1, CH, P, P).transpose(0, 2, 1, 3).reshape(-1, P, CH * P)


def _pairs(x, y):
    return [z for pair in zip(x, y) for z in pair]


def _wide(w):
    return w.reshape(2, 4, P, -1, WIDE).transpose(3, 0, 2, 1, 4).reshape(-1, 2, P, 4 * WIDE)


def _channels(x):
    return x.reshape(x.shape[0], -1, P).transpose(2, 1, 0)


def _column(v):
    return v.reshape(-1, P).T


def kernel(**inputs):
    import concourse.bacc as bacc
    from concourse import mybir
    from concourse.bass_utils import run_bass_kernel_spmd as run

    x = {k: np.asarray(v) for k, v in inputs.items()}
    F32 = np.float32

    chunks = []
    for l in range(DEPTH):
        w = _blocks(x["w_in"][l])
        parts = [w[32:36], w[28:32], w[0:4], w[4:8], w[8:12], w[12:20]]
        parts += _pairs(w[52:60], _blocks(x["conv_proj"][l]))
        parts += [w[20:28]]
        parts += _pairs(w[44:52], _blocks(x["ret_proj"][l]))
        parts += [_blocks(x["s5_glu_w"][l])]
        parts += _pairs(w[36:44], _blocks(x["s5_proj"][l]))
        parts += [_blocks(x["w_out"][l])]
        if l == 0:
            parts += _pairs(_blocks(x["ffn_w_gate"][0]), _blocks(x["ffn_w_up"][0]))
            parts += [_blocks(x["ffn_w_down"][0])]
        chunks.append(_stream(parts))
    experts = []
    for e in range(NEXP):
        experts.append(np.stack([_wide(x["moe_w_gate"][0, e]), _wide(x["moe_w_up"][0, e])], axis=1).reshape(GU, P, 2048))
        experts.append(x["moe_w_down"][0, e].reshape(DN, 2, P, D).transpose(0, 2, 1, 3).reshape(DN, P, 2048))

    def groups(v):
        v = v.reshape((2, GJ) + v.shape[1:])
        return np.moveaxis(v, 1, 2).reshape((P, GJ) + v.shape[3:])

    f = {}
    f["weights"] = np.concatenate(chunks)
    f["experts"] = np.concatenate(experts)
    f["xT"] = np.concatenate([_channels(x["x_prompt"][0]), _channels(x["x_sample"][:, 0])], axis=2)
    f["vecs"] = np.concatenate([c for l in range(DEPTH) for c in (
        _column(x["norm_mix_g"][l]), _column(x["norm_ffn_g"][l]), _column(x["conv_pw_b"][l]),
        _channels(x["conv_dw_w"][l]).reshape(P, -1), _column(x["conv_dw_b"][l]), _column(x["conv_ln_g"][l]),
        _column(x["conv_ln_b"][l]), _column(x["s5_glu_b"][l]))] + [_column(x["norm_final_g"])], axis=1)
    rows = [x["s5_lambda_re"], x["s5_lambda_im"], np.repeat(x["s5_log_dt"][:, :, None], 64, axis=2)]
    f["lam"] = np.stack([np.concatenate([groups(r[l]) for l in range(DEPTH)], axis=1) for r in rows], axis=1)
    f["dskip"] = np.stack([x["s5_d"][l].reshape(G, GP).T for l in range(DEPTH)], axis=1)
    f["bc"] = np.stack([np.concatenate([
        groups(x["s5_b_re"][l]).reshape(P, -1), groups(x["s5_b_im"][l]).reshape(P, -1),
        groups(x["s5_c_re"][l].transpose(0, 2, 1)).reshape(P, -1), groups(x["s5_c_im"][l].transpose(0, 2, 1)).reshape(P, -1),
    ], axis=1) for l in range(DEPTH)])
    f["h0"] = np.stack([np.stack([groups(x[n][l].transpose(1, 2, 0)) for n in ("state_s5_re", "state_s5_im")], axis=1)
                        for l in range(DEPTH)])
    f["convst"] = np.stack([x["state_conv"][l].reshape(NS, TAPS - 1, 4, P).transpose(3, 2, 0, 1) for l in range(DEPTH)])
    f["sret"] = x["state_ret"]
    f["router"] = x["moe_router"][0].reshape(KD, P, NEXP).transpose(1, 0, 2)

    half = P // 2
    freqs = F32(10000.0) ** (-np.arange(half, dtype=F32) / F32(half))
    pos = np.concatenate([np.arange(SEQ), np.full(NS, 2048)]).astype(F32)
    ang = (pos[None, :] * freqs[:, None]).astype(F32).astype(np.float64)
    cos = np.concatenate([np.cos(ang), np.cos(ang)])
    sin = np.concatenate([np.sin(ang), -np.sin(ang)])
    scale = P ** -0.5
    f["rope"] = np.stack([cos, sin, cos * scale, sin * scale], axis=1).astype(F32)
    gamma = 1.0 - 2.0 ** (-5.0 - np.arange(HEADS))
    j, i = np.arange(P)[:, None], np.arange(SEQ)[None, :]
    f["decay"] = np.stack([np.where(i >= j, g ** np.maximum(i - j, 0), 0.0) for g in gamma], axis=1).astype(F32)
    f["kdec"] = np.stack([np.stack([g ** (SEQ - 1 - it * P - np.arange(P)) for g in gamma], axis=1) for it in range(2)], axis=1).astype(F32)
    f["ident"] = np.eye(P, dtype=F32)
    f["tri"] = np.triu(np.ones((P, P), F32), 1)
    f["iota"] = np.tile(np.arange(CAP, dtype=F32), (P, 1))

    outs = {"y": (P, KD, T), "h_p": (DEPTH, P, 2, GJ), "h_s": (DEPTH, P, 2, GJ, NS),
            "ret_p": (DEPTH, HEADS, P, DV), "ret_s": (DEPTH, NS, HEADS, P, DV),
            "conv_p": (DEPTH, P, 4, TAPS - 1), "conv_s": (DEPTH, P, 4, NS, TAPS - 1)}

    nc = bacc.Bacc("TRN2", target_bir_lowering=False, num_devices=1)
    arrays, args = {}, {}
    for name, v in f.items():
        v = np.ascontiguousarray(v)
        arrays["in_" + name] = v
        args[name] = nc.dram_tensor("in_" + name, v.shape, mybir.dt.from_np(v.dtype), kind="ExternalInput").ap()
    for name, shape in outs.items():
        args[name] = nc.dram_tensor("out_" + name, shape, mybir.dt.float32, kind="ExternalOutput").ap()
    build(nc, args)
    r = run(nc, [arrays], core_ids=[0]).results[0]
    o = {name: r["out_" + name] for name in outs}

    y = o["y"].transpose(2, 1, 0).reshape(T, D)

    def ungroup(v):
        return v.reshape(DEPTH, 2, 64, GJ).transpose(0, 1, 3, 2).reshape(DEPTH, G, 64)

    h_p = [ungroup(o["h_p"][:, :, r]).reshape(DEPTH, 1, G, 64) for r in range(2)]
    h_s = [np.stack([ungroup(o["h_s"][:, :, r, :, b]) for b in range(NS)], axis=1) for r in range(2)]
    conv_p = o["conv_p"].transpose(0, 3, 2, 1).reshape(DEPTH, 1, TAPS - 1, 4 * P)
    conv_s = o["conv_s"].transpose(0, 3, 4, 2, 1).reshape(DEPTH, NS, TAPS - 1, 4 * P)
    return (y[None, :SEQ], y[SEQ:, None, :], h_p[0], h_p[1], o["ret_p"].reshape(DEPTH, 1, HEADS, P, DV), conv_p,
            h_s[0], h_s[1], o["ret_s"], conv_s)
```

```python
import numpy as np

P = 128
D = 1024
KD = D // P
SEQ = 256
NS = 8
T = SEQ + NS
DEPTH = 2
G = 32
GP = 16
GJ = G // 2
S = 8
NC = SEQ // S
HEADS = 4
DV = 256
TAPS = 31
F_DENSE = 2816 // P
F_EXP = 3584 // P
NEXP = 8
CAP = 112
EPS = 1e-6
NBANK = 8
CH = 8
RING = 5
HIGHS = 3
WIDE = 512
E_TILES = 3584 // WIDE
GU = 4 * E_TILES
DN = F_EXP // 2
E_CHUNKS = GU + DN
MRING = 7
HRING = 6
AHEAD = 4
UT = [(0, 128), (128, 128), (256, 8)]
BIG = 4096.0

V_GM, V_GF, V_PWB, V_DWW, V_DWB, V_LNG, V_LNB, V_GLB = 0, 8, 16, 24, 148, 152, 156, 160
V_L = 164
V_FIN = DEPTH * V_L
NV = V_FIN + 8


def tile_order():
    o = []
    for l in range(DEPTH):
        def add(name, n, blocks=0):
            for i in range(n):
                o.append(((l, name, i), blocks))
        if l == 0:
            add("ms1", 1)
        for name, n in (("cb", 4), ("ca", 4), ("zs", 4), ("q", 4), ("k", 4), ("v", 8)):
            add(name, n, KD)
        add("vt", 4); add("vs", 2); add("kt", 2); add("ks", 1)
        add("win", 8); add("kk", 8)
        for h in range(HEADS):
            o += [((l, "sc", h), 0), ((l, "ou", h), 0), ((l, "st", h), 0)]
        add("si", 4); add("cm", 1); add("cv", 1)
        for d in range(KD):
            o += [((l, "gc", d), KD)]
            if d > 0:
                o += [((l, "os", d - 1), 0)]
            o += [((l, "pc", d), 4), ((l, "oa", d), 0), ((l, "ob", d), 0)]
        o += [((l, "os", KD - 1), 0)]
        add("gm", 4); add("gv", 4); add("y", 8)
        add("gg", 8, KD)
        add("yt", 4)
        for d in range(KD):
            o += [((l, "gr", d), KD), ((l, "pr", d), KD)]
        add("gl", 4, 4)
        for d in range(KD):
            o += [((l, "gs", d), KD), ((l, "ps", d), 4)]
        for d in range(KD):
            o += [((l, "wo", d), KD)]
            if d == 0:
                add("ms2", 1)
        if l == 0:
            for f in range(F_DENSE):
                o += [((l, "fg", f), KD), ((l, "fu", f), KD)]
            for d in range(KD):
                o += [((l, "dn", d), F_DENSE)]
                if d == 0:
                    o += [((l + 1, "ms1", 0), 0)]
    l = DEPTH - 1
    o += [((l, "lg", i), 0) for i in range(3)]
    o += [((l, "tt", i), 0) for i in range(6)]
    o += [((l, "po", 0), 0)]
    return o


def sum_of(key):
    l, name, _ = key
    return {"wo": (l, "ms2", 0), "dn": (l + 1, "ms1", 0)}.get(name)


def tile_counts():
    place, done, chunk = {}, {}, []
    n = b = 0
    for i, (key, blocks) in enumerate(tile_order()):
        place[key] = i
        if key[1] in ("ms1", "ms2") and i > 0:
            continue
        for x in range(blocks):
            b += 1
            if b % CH == 0:
                if x < blocks - 1:
                    n += 1
                    chunk.append(n)
                else:
                    chunk.append(n + 1)
        n += 1
        done[key] = n
        if sum_of(key) and key[2] == KD - 1:
            n += 1
            done[sum_of(key)] = n
    assert b % CH == 0
    return place, done, chunk, n


def chunk_of_tile():
    last, b = {}, 0
    for key, blocks in tile_order():
        b += blocks
        last[key] = (b + CH - 1) // CH - 1
    return last


def part_order():
    o = []
    for l in range(DEPTH):
        names = [("u", KD), ("c", 4), ("r", KD), ("y", 4), ("g", 4), ("m", KD)]
        if l == 0:
            names += [("n", KD), ("h", F_DENSE)]
        o += [(l, name, k) for name, n in names for k in range(n)]
    return {key: i + 1 for i, key in enumerate(o)}


def build(nc, a):
    import concourse.bass as bass
    from concourse import mybir
    from contextlib import ExitStack

    F = mybir.dt.float32
    F32R = mybir.dt.float32r
    I32 = mybir.dt.int32
    U32 = mybir.dt.uint32
    ACT = mybir.ActivationFunctionType
    ALU = mybir.AluOpType
    AX = mybir.AxisListType.X
    PLACE, DONE, CHUNK_DONE, MM_BASE = tile_counts()
    N_CHUNKS = len(CHUNK_DONE)
    CHUNK_OF = chunk_of_tile()
    PART = part_order()

    with ExitStack() as ctx:
        start_of = {}

        def sb(name, shape, dt=F):
            start_of[name] = -(-nc.sbuf_base // 32) * 32
            return ctx.enter_context(nc.sbuf_tensor(name, shape, dt))

        def parts_of(name, width):
            return nc.alloc_sbuf_tensor_at(name + "_parts", [P, width], F32R, offset=start_of[name])

        def sem(name):
            return ctx.enter_context(nc.semaphore(name))

        xT = sb("xT", [P, KD, T])
        uT = sb("uT", [P, KD, T])
        uT_hi = sb("uT_hi", [P, KD, T], F32R)
        ring = sb("ring", [P, (RING + HIGHS) * CH * P])
        s5m = sb("s5m", [P, 15648])
        zone = sb("zone", [P, 10584])
        work = sb("work", [P, 6656])
        sq = sb("sq", [P, 1056])
        rstd = sb("rstd", [P, 2, T])
        gate = sb("gate", [P, 2, T])
        tmp = sb("tmp", [P, 2, T])
        table = sb("table", [P, HEADS * SEQ])
        kdec = sb("kdec", [P, 2, HEADS])
        ident = sb("ident", [P, P])
        tri = sb("tri", [P, P])
        ones = sb("ones", [P, P])
        iota = sb("iota", [P, CAP])
        vecs = sb("vecs", [P, NV])
        eps = sb("eps", [P, 1])
        lam = sb("lam", [P, 3, DEPTH * GJ])
        lw = sb("lw", [P, 16, DEPTH * GJ])
        dskip = sb("dskip", [GP, DEPTH, G])
        l8 = sb("l8", [P, 4, GJ])
        rec = sb("rec", [P, 3, 2, GJ])
        qs = sb("qs", [P, HEADS, NS])
        router = sb("router", [P, KD, NEXP])

        rope = table[:, 0:2 * T].rearrange("p (w t) -> p w t", w=2)
        decay = table[:, :].rearrange("p (h t) -> p h t", h=HEADS)
        toep = s5m[:, 0:4096].rearrange("p (g x) -> p g x", g=G)
        gb = s5m[:, 0:4096].rearrange("p (j r s q) -> p j r s q", j=GJ, r=2, s=S)
        gb2 = s5m[:, 0:4096]
        winT = s5m[:, 4096:8192]
        clr = s5m[:, 8192:10496].rearrange("p (j x) -> p j x", j=GJ)
        cli = s5m[:, 10496:12800].rearrange("p (j x) -> p j x", j=GJ)
        xin = s5m[:, 12800:14336].rearrange("p (g x) -> p g x", g=G)
        hst = s5m[:, 14336:15648].rearrange("p (r j c) -> p r j c", r=2, j=GJ)
        sigb = zone[:, 0:1056].rearrange("p (m t) -> p m t", m=4)
        xc = zone[:, 1056:2200].rearrange("p (m t) -> p m t", m=4)
        yg = zone[:, 1056:2112].rearrange("p (m t) -> p m t", m=4)
        xs = zone[:, 2200:3192].rearrange("p (m b k) -> p m b k", m=4, b=NS)
        cT = zone[:, 3192:4248].rearrange("p (m t) -> p m t", m=4)
        qT = zone[:, 4248:5304].rearrange("p (h t) -> p h t", h=HEADS)
        kT = zone[:, 5304:6360].rearrange("p (h t) -> p h t", h=HEADS)
        mT = zone[:, 4248:6360].rearrange("p (m t) -> p m t", m=KD)
        vT = zone[:, 6360:8472].rearrange("p (m t) -> p m t", m=KD)
        vtok = zone[:, 8472:10520].rearrange("p (i x) -> p i x", i=2)
        yst = s5m[:, 4096:8192].rearrange("c (s g q) -> c s g q", s=S, g=G)
        hT = zone[:, 0:F_DENSE * T].rearrange("p (f t) -> p f t", f=F_DENSE)
        kd = work[:, 0:1024].rearrange("p (i x) -> p i x", i=2)
        pt = work[:, 1024:1792].rearrange("p (b x) -> p b x", b=2)
        si = work[:, 0:1536].rearrange("p (r j c) -> p r j c", r=2, j=GJ)
        kst = work[:, 1792:2304]
        kmask = work[:, 2304:3328].rearrange("p (b x) -> p b x", b=2)
        vst = work[:, 3328:4352]
        sring = work[:, 4352:6400].rearrange("p (b h x) -> p b h x", b=2, h=HEADS)
        hnew = work[:, 6400:6656].rearrange("p (r j b) -> p r j b", r=2, j=GJ)
        stst = sq[:, 0:1024].rearrange("p (h x) -> p h x", h=HEADS)
        bc = work[:, 0:1024].rearrange("p (w j q) -> p w j q", w=4, j=GJ)
        bb = work[:, 1024:1536].rearrange("p (r j q) -> p r j q", r=2, j=GJ)
        pa = work[:, 1536:1824].rearrange("p (r k j) -> p r k j", r=2, k=9)
        pd = work[:, 1824:2080].rearrange("p (r k j) -> p r k j", r=2, k=8)
        pw = work[:, 2080:2208].rearrange("p (r k j) -> p r k j", r=2, k=4)
        pt1 = work[:, 2304:4608]
        dd = work[0:GP, 4608:5120].rearrange("p (g q) -> p g q", g=G)
        utok = work[:, 0:3072].rearrange("p (i x) -> p i x", i=3)
        sel = work[:, 3072:3072 + 3 * CAP].rearrange("p (i c) -> p i c", i=3)
        selw = work[:, 3408:3408 + 3 * CAP].rearrange("p (i c) -> p i c", i=3)
        selT = work[:, 3744:4008]
        ytok = work[:, 4904:5928]
        hm = s5m[:, 14336:15360].rearrange("p (b x) -> p b x", b=2)
        rt = work[:, 5928:6408].rearrange("p (w i e) -> p w i e", i=3, e=8)
        rti = sq[:, 0:24].bitcast(U32).rearrange("p (i e) -> p i e", i=3)
        items_t = sq[:, 24:25].bitcast(I32)
        slotx = work[:, 6408:6483].rearrange("p (i c) -> p i c", i=3)
        combx = work[:, 6483:6558].rearrange("p (i c) -> p i c", i=3)
        cur = work[:, 6558:6567].rearrange("p (w i) -> p w i", w=3)
        hfin = sb("hfin", [P, 2, GJ])
        HE = F_EXP * CAP

        uT_lo = parts_of("uT", KD * T)[:, :].rearrange("p (m t) -> p m t", m=KD)
        s5m_parts = parts_of("s5m", 15648)
        ring_parts = parts_of("ring", (RING + HIGHS) * CH * P)
        zone_parts = parts_of("zone", 10584)
        work_parts = parts_of("work", 6656)
        table_parts = parts_of("table", HEADS * SEQ)
        sq_parts = parts_of("sq", 1056)

        def blocks(of, lo, n):
            return of[:, lo:lo + n * T].rearrange("p (m t) -> p m t", m=n)

        cT_hi, cT_lo = blocks(sq_parts, 0, 4), blocks(zone_parts, 3192, 4)
        vT_hi, vT_lo = blocks(work_parts, 0, KD), blocks(zone_parts, 6360, KD)
        yg_hi, yg_lo = blocks(zone_parts, 3192, 4), blocks(zone_parts, 8472, 4)
        glu_hi, glu_lo = blocks(zone_parts, 9528, 4), blocks(zone_parts, 0, 4)
        mT_hi, mT_lo = blocks(zone_parts, 6360, KD), blocks(zone_parts, 4248, KD)
        hT_lo = blocks(zone_parts, 0, F_DENSE)
        behind = (10584 - F_DENSE * T) // T
        hT_hi = blocks(zone_parts, F_DENSE * T, behind)
        hT_hi2 = blocks(sq_parts, 0, F_DENSE - behind)
        PARTS = {"u": (uT_hi, uT_lo), "n": (uT_hi, uT_lo), "c": (cT_hi, cT_lo), "r": (vT_hi, vT_lo),
                 "y": (yg_hi, yg_lo), "g": (glu_hi, glu_lo), "m": (mT_hi, mT_lo)}

        def parts(name, k):
            if name == "h":
                high = hT_hi[:, k, :] if k < behind else hT_hi2[:, k - behind, :]
                return high, hT_lo[:, k, :]
            high, low = PARTS[name]
            return high[:, k, :], low[:, k, :]

        def weights(c, of):
            s = c % RING
            return of[:, s * CH * P:(s + 1) * CH * P]

        def weights_hi(c):
            s = RING + c % HIGHS
            return ring_parts[:, s * CH * P:(s + 1) * CH * P]

        xg_hi = work_parts[:, 4008:4008 + KD * CAP].rearrange("p (k c) -> p k c", k=KD)
        xg_lo = table_parts[:, 0:KD * CAP].rearrange("p (k c) -> p k c", k=KD)
        hE_hi = zone_parts[:, 0:HE].rearrange("p (f c) -> p f c", f=F_EXP)
        hE_lo = zone_parts[:, HE:2 * HE].rearrange("p (f c) -> p f c", f=F_EXP)

        def slot(c, of):
            s = c % MRING
            return of[:, s * 2048:(s + 1) * 2048]

        def high_slot(c):
            s = c % HRING
            if s < 4:
                return ring_parts[:, s * 2048:(s + 1) * 2048]
            o = 2 * HE + (s - 4) * 2048
            return zone_parts[:, o:o + 2048]

        def f32(ap):
            return ap.bitcast(F)

        bank = [ctx.enter_context(nc.psum_tensor(f"bank{b}", [P, 512], F)) for b in range(NBANK)]

        zscr = nc.dram_tensor("zscr", [G * GP, T], F, kind="Internal").ap()
        kscr = nc.dram_tensor("kscr", [G, GP, 2 * P], F, kind="Internal").ap()

        consts_in = sem("consts_in")
        ones_set = sem("ones_set")
        loaded = [sem(f"loaded{s}") for s in range(RING)]
        mloaded = [sem(f"mloaded{s}") for s in range(MRING)]
        mm_done = sem("mm_done")
        evicted = [sem(f"bank_evicted{b}") for b in range(NBANK)]
        dve_order = sem("dve_order")
        pool_order = sem("pool_order")
        squares = sem("squares_done")
        x_squares = sem("x_squares")
        x_in = sem("x_in")
        lam_in = sem("lam_in")
        std_done = sem("std_done")
        u_ready = sem("u_ready")
        x_high = sem("x_high")
        x_low = sem("x_low")
        c_act = sem("c_act")
        table_in = sem("table_in")
        lam_ready = sem("lam_ready")
        lam_act = sem("lam_act")
        conv_step = sem("conv_step")
        conv_done = sem("conv_done")
        conv_state_in = sem("conv_state_in")
        conv_state_out = sem("conv_state_out")
        l8_ready = sem("l8_ready")
        gb_ready = sem("gb_ready")
        kmat_ready = sem("kmat_ready")
        kscr_out = sem("kscr_out")
        toep_in = sem("toep_in")
        bc_in = sem("bc_in")
        zero_out = sem("zero_out")
        zscr_out = sem("zscr_out")
        xin_in = sem("xin_in")
        h0_in = sem("h0_in")
        h_ready = sem("h_ready")
        hstate_out = sem("hstate_out")
        kmask_ready = sem("kmask_ready")
        s_in = [sem(f"s_in{b}") for b in range(2)]
        s_out = [sem(f"s_out{b}") for b in range(2)]
        st_out = sem("st_out")
        qs_ready = sem("qs_ready")
        cn_ready = sem("cn_ready")
        gated = sem("gated")
        gelu_done = sem("gelu_done")
        glu_done = sem("glu_done")
        merged = sem("merged")
        route_act = sem("route_act")
        route_ready = sem("route_ready")
        items_ready = sem("items_ready")
        sel_ready = sem("sel_ready")
        cur_ready = sem("cur_ready")
        misc_done = sem("misc_done")
        high_done = sem("high_done")
        low_done = sem("low_done")
        hidden_high = sem("hidden_high")
        gathered_high = sem("gathered_high")
        y_out = sem("y_out")
        xin_zero = sem("xin_zero")
        x_final = sem("x_final")

        def at(key):
            return bank[PLACE[key] % NBANK]

        def out_of(key):
            return evicted[PLACE[key] % NBANK], PLACE[key] // NBANK + 1

        def freed(key):
            return evicted[PLACE[key] % NBANK]

        def vec(l, col, m):
            c = l * V_L + col + m
            return vecs[:, c:c + 1]

        BASE = [sum(1 for i in range(len(PLACE)) if i % NBANK == b) + (b in (1, 3)) for b in range(NBANK)]
        USES = [4 + 2, 3 + 1, 4 + 2, 3 + 1, 4 + 2, 3 + 1 + 2, 1, 1]
        SCATTER = (0, 2, 4, 5)
        SCATTER_USE = (4, 4, 4, 4)
        M_ONEHOT, M_GATHER, M_SCATTER = E_TILES, E_TILES + 1, E_TILES + 3
        MISC = M_SCATTER + KD
        MISC0 = 2
        TURNS = E_CHUNKS // MRING

        block = ctx.enter_context(nc.Block())

        @block.sync
        def _(sp):
            sp.dma_start(lam[:, :, :], a["lam"]).then_inc(lam_in, 16)
            sp.dma_start(xT[:, :, :], a["xT"]).then_inc(x_in, 16)
            for n in range(2):
                sp.dma_start(weights(n, ring), a["weights"][n]).then_inc(loaded[n], 16)
            loads = [(vecs[:, :], a["vecs"]), (kdec[:, :, :], a["kdec"]),
                     (ident[:, :], a["ident"]), (tri[:, :], a["tri"]), (iota[:, :], a["iota"]),
                     (dskip[:, :, :], a["dskip"]), (router[:, :, :], a["router"])]
            for dst, src in loads:
                sp.dma_start(dst, src).then_inc(consts_in, 16)
            sp.dma_start(rope, a["rope"]).then_inc(table_in, 16)

            for n in range(2, N_CHUNKS):
                if n >= RING:
                    sp.wait_ge(mm_done, CHUNK_DONE[n - RING])
                sp.dma_start(weights(n, ring), a["weights"][n]).then_inc(loaded[n % RING], 16)
                for l in range(DEPTH):
                    if n == CHUNK_OF[(l, "v", 3)] + RING:
                        sp.wait_ge(*out_of((l, "k", 3)))
                        sp.dma_start(decay, a["decay"]).then_inc(table_in, 16)
                if n == CHUNK_OF[(0, "pc", 0)] + RING:
                    sp.wait_ge(*out_of((0, "sc", HEADS - 1)))
                    sp.dma_start(rope, a["rope"]).then_inc(table_in, 16)

            sp.wait_ge(mm_done, DONE[(DEPTH - 1, "yt", 3)])
            sp.wait_ge(hstate_out, 32 * DEPTH)
            for s in range(MRING):
                sp.dma_start(slot(s, s5m), a["experts"][s]).then_inc(mloaded[s], 16)
            sp.wait_ge(items_ready, 1)
            items = sp.value_load(items_t[0:1, 0:1], min_val=NEXP, max_val=3 * NEXP)
            with sp.Fori(0, items * TURNS - 1) as q:
                for s in range(MRING):
                    sp.wait_ge(mm_done, q * MRING + MM_BASE + s + 1)
                    row = ((q + 1) % (NEXP * TURNS)) * MRING + s
                    sp.dma_start(slot(s, s5m), a["experts"][bass.ds(row, 1)].rearrange("o p x -> (o p) x")
                                 ).then_inc(mloaded[s], 16)
            for s in range(AHEAD):
                sp.wait_ge(mm_done, items * E_CHUNKS + MM_BASE - MRING + s + 1)
                sp.dma_start(slot(s, s5m), a["experts"][s]).then_inc(mloaded[s], 16)

            for lo, hi in ((0, 4), (4, 7), (7, 8)):
                sp.wait_ge(x_final, hi)
                sp.dma_start(a["y"][:, lo:hi, :], uT[:, lo:hi, :]).then_inc(y_out, 16)
            sp.wait_ge(y_out, 48)

        @block.tensor
        def _(pe):
            state = {"tile": 0, "block": 0}

            def open_tile(key):
                n = state["tile"]
                assert PLACE[key] == n, (key, n)
                state["tile"] += 1
                if n >= NBANK:
                    pe.wait_ge(evicted[n % NBANK], n // NBANK)
                return bank[n % NBANK]

            def split_product(out, left, right, first, last):
                pe.matmul(out, left[0], right[1], start=first, stop=False)
                pe.matmul(out, left[1], right[0], start=False, stop=False)
                return pe.matmul(out, left[0], right[0], start=False, stop=last)

            seen = set()

            def weight_tile(key, name, n_blocks):
                out = open_tile(key)
                for k in range(n_blocks):
                    b = state["block"]
                    c = b // CH
                    if b % CH == 0:
                        pe.wait_ge(low_done, c + 1)
                    part = (key[0], name, k)
                    if part not in seen:
                        seen.add(part)
                        pe.wait_ge(x_low, PART[part])
                    x = b % CH
                    w = slice(x * P, (x + 1) * P)
                    mm = split_product(out[:, 0:T], (weights_hi(c)[:, w], weights(c, ring_parts)[:, w]),
                                       parts(name, k), k == 0, k == n_blocks - 1)
                    state["block"] += 1
                    if (b + 1) % CH == 0 and k < n_blocks - 1:
                        mm.then_inc(mm_done, 1)
                mm.then_inc(mm_done, 1)

            def sum_tile(key, terms, n):
                out = open_tile(key)
                for i in range(n):
                    mm = pe.matmul(out[:, 0:T], ones[:, :], terms(i), start=(i == 0), stop=(i == n - 1))
                mm.then_inc(mm_done, 1)

            def sum_open(key):
                state["sum"] = open_tile(key)

            def sum_feed(norm, k):
                pe.wait_ge(x_squares, KD * norm + k + 1)
                mm = pe.matmul(state["sum"][:, 0:T], ones[:, :], uT[:, k, :], start=(k == 0), stop=(k == KD - 1))
                if k == KD - 1:
                    mm.then_inc(mm_done, 1)

            def stream_tiles(l, name, x, n_blocks, norm):
                for d in range(KD):
                    weight_tile((l, name, d), x, n_blocks)
                    if d == 0:
                        sum_open(sum_of((l, name, 0)))
                    else:
                        sum_feed(norm, d - 1)
                sum_feed(norm, KD - 1)

            pe.wait_ge(ones_set, 2)
            for l in range(DEPTH):
                if l == 0:
                    sum_open((l, "ms1", 0))
                    for k in range(KD):
                        sum_feed(0, k)
                    pe.wait_ge(consts_in, 16 * 7)
                for name, n in (("cb", 4), ("ca", 4), ("zs", 4), ("q", 4), ("k", 4), ("v", 8)):
                    for m in range(n):
                        weight_tile((l, name, m), "u", KD)
                for i in range(4):
                    it, half = i // 2, i % 2
                    pe.wait_ge(*out_of((l, "v", 4 * half + 3)))
                    out = open_tile((l, "vt", i))
                    for m in range(4):
                        mm = pe.transpose(out[:, m * P:(m + 1) * P], vT[:, 4 * half + m, it * P:(it + 1) * P], ident[:, :])
                    mm.then_inc(mm_done, 1)
                for half in range(2):
                    out = open_tile((l, "vs", half))
                    for m in range(4):
                        mm = pe.transpose(out[0:NS, m * P:(m + 1) * P], vT[:, 4 * half + m, SEQ:T], ident[:, :])
                    mm.then_inc(mm_done, 1)
                pe.wait_ge(*out_of((l, "k", 3)))
                pe.wait_ge(qs_ready, l + 1)
                for i in range(2):
                    out = open_tile((l, "kt", i))
                    for h in range(HEADS):
                        mm = pe.transpose(out[:, h * P:(h + 1) * P], kT[:, h, i * P:(i + 1) * P], ident[:, :])
                    mm.then_inc(mm_done, 1)
                out = open_tile((l, "ks", 0))
                for h in range(HEADS):
                    mm = pe.transpose(out[0:NS, h * P:(h + 1) * P], kT[:, h, SEQ:T], ident[:, :])
                mm.then_inc(mm_done, 1)
                pe.wait_ge(gb_ready, l + 1)
                for i in range(8):
                    out = open_tile((l, "win", i))
                    for x in range(4):
                        c = (4 * i + x) * P
                        mm = pe.transpose(out[:, x * P:(x + 1) * P], gb2[:, c:c + P], ident[:, :])
                    mm.then_inc(mm_done, 1)
                for i in range(8):
                    out = open_tile((l, "kk", i))
                    g2 = i // 4
                    lo, hi = 64 * g2, 64 * g2 + 64
                    for x in range(4):
                        j = 4 * (i % 4) + x
                        pe.matmul(out[0:GP, x * P:(x + 1) * P], bb[lo:hi, 0, j, :], clr[lo:hi, j, 0:P],
                                  start=True, stop=False)
                        mm = pe.matmul(out[0:GP, x * P:(x + 1) * P], bb[lo:hi, 1, j, :], cli[lo:hi, j, 0:P],
                                       start=False, stop=True)
                    mm.then_inc(mm_done, 1)
                pe.wait_ge(*out_of((l, "kt", 1)))
                pe.wait_ge(*out_of((l, "vt", 3)))
                pe.wait_ge(*out_of((l, "vt", 2)))
                pe.wait_ge(*out_of((l, "vt", 1)))
                pe.wait_ge(*out_of((l, "vt", 0)))
                pe.wait_ge(*out_of((l, "kt", 0)))
                for h in range(HEADS):
                    out = open_tile((l, "sc", h))
                    pe.matmul(out[:, 0:SEQ], kT[:, h, 0:P], qT[:, h, 0:SEQ], start=True, stop=True)
                    pe.matmul(out[:, SEQ:SEQ + P], kT[:, h, P:SEQ], qT[:, h, P:SEQ], start=True, stop=True
                              ).then_inc(mm_done, 1)
                    out = open_tile((l, "ou", h))
                    pe.wait_ge(*out_of((l, "sc", h)))
                    for half in range(2):
                        c = h * DV + half * P
                        pe.matmul(out[:, half * SEQ:(half + 1) * SEQ], vtok[:, 0, c:c + P], pt[:, h % 2, 0:SEQ],
                                  start=True, stop=False)
                        mm = pe.matmul(out[:, half * SEQ + P:(half + 1) * SEQ], vtok[:, 1, c:c + P],
                                       pt[:, h % 2, SEQ:SEQ + P], start=False, stop=True)
                    mm.then_inc(mm_done, 1)
                    out = open_tile((l, "st", h))
                    for i in range(2):
                        mm = pe.matmul(out[:, 0:DV], kd[:, i, h * P:(h + 1) * P], vtok[:, i, h * DV:(h + 1) * DV],
                                       start=(i == 0), stop=(i == 1))
                    mm.then_inc(mm_done, 1)
                pe.wait_ge(xin_in, 160 * (l + 1))
                for i in range(8):
                    pe.wait_ge(*out_of((l, "win", i)))
                for i in range(4):
                    out = open_tile((l, "si", i))
                    for x in range(8):
                        j, ri = 4 * i + x // 2, x % 2
                        for g2 in range(2):
                            c = (2 * j + ri) * P + 64 * g2
                            mm = pe.matmul(out[64 * g2:64 * g2 + 64, x * 48:(x + 1) * 48], winT[:, c:c + 64],
                                           xin[:, g2 * GJ + j, :], start=True, stop=True)
                    mm.then_inc(mm_done, 1)
                pe.wait_ge(conv_done, l + 1)
                sum_tile((l, "cm", 0), lambda m: cT[:, m, :], 4)
                pe.wait_ge(squares, 5 * l + 1)
                sum_tile((l, "cv", 0), lambda m: sq[:, m * T:(m + 1) * T], 4)

                def sample_output(b):
                    out = open_tile((l, "os", b))
                    pe.wait_ge(*out_of((l, "oa", b)))
                    pe.wait_ge(*out_of((l, "ob", b)))
                    for x in range(KD):
                        h, half = x // 2, x % 2
                        mm = pe.matmul(out[:, x:x + 1], sring[:, b % 2, h, half * P:(half + 1) * P],
                                       qs[:, h, b:b + 1], start=True, stop=True)
                    mm.then_inc(mm_done, 1)

                for b in range(NS):
                    weight_tile((l, "gc", b), "u", KD)
                    if b > 0:
                        sample_output(b - 1)
                    weight_tile((l, "pc", b), "c", 4)
                    pe.wait_ge(kmask_ready, NS * l + b + 1)
                    for half, name in ((0, "oa"), (1, "ob")):
                        out = open_tile((l, name, b))
                        for x in range(2):
                            h = 2 * half + x
                            mm = pe.matmul(out[:, x * DV:(x + 1) * DV], kmask[0:NS, b % 2, h * P:(h + 1) * P],
                                           vst[0:NS, h * DV:(h + 1) * DV], start=True, stop=True)
                        mm.then_inc(mm_done, 1)
                sample_output(NS - 1)
                for h in range(HEADS):
                    pe.wait_ge(*out_of((l, "ou", h)))
                for b in range(NS):
                    pe.wait_ge(*out_of((l, "os", b)))
                for h in range(HEADS):
                    sum_tile((l, "gm", h), lambda x: vT[:, 2 * h + x, :], 2)
                for h in range(HEADS):
                    pe.wait_ge(squares, 5 * l + 2 + h)
                    c = (h % 2) * 2 * T
                    sum_tile((l, "gv", h), lambda x: sq[:, c + x * T:c + (x + 1) * T], 2)
                pe.wait_ge(h_ready, l + 1)
                pe.wait_ge(toep_in, 128 * (l + 1))
                for i in range(8):
                    out = open_tile((l, "y", i))
                    g2 = i // 4
                    lo, hi = 64 * g2, 64 * g2 + 64
                    for x in range(4):
                        g = 4 * i + x
                        j = g % GJ
                        o = out[0:NC + NS, x * P:(x + 1) * P]
                        pe.matmul(o, xin[:, g, 0:NC + NS], toep[:, g, :], start=True, stop=False)
                        pe.matmul(o, hst[lo:hi, 0, j, 0:NC + NS], clr[lo:hi, j, GP:GP + P], start=False, stop=False)
                        mm = pe.matmul(o, hst[lo:hi, 1, j, 0:NC + NS], cli[lo:hi, j, GP:GP + P], start=False, stop=True)
                    mm.then_inc(mm_done, 1)
                for m in range(KD):
                    weight_tile((l, "gg", m), "u", KD)
                for i in range(8):
                    pe.wait_ge(*out_of((l, "y", i)))
                for m in range(4):
                    out = open_tile((l, "yt", m))
                    for s in range(S):
                        lo, n = (0, NC + NS) if s == 0 else (NS + s * NC, NC)
                        mm = pe.transpose(out[:, lo:lo + n], yst[0:n, s, 8 * m:8 * m + 8, :].rearrange("c g q -> c (g q)"),
                                          ident[0:n, 0:n])
                    mm.then_inc(mm_done, 1)
                for d in range(KD):
                    weight_tile((l, "gr", d), "u", KD)
                    weight_tile((l, "pr", d), "r", KD)
                for m in range(4):
                    weight_tile((l, "gl", m), "y", 4)
                for d in range(KD):
                    weight_tile((l, "gs", d), "u", KD)
                    weight_tile((l, "ps", d), "g", 4)
                stream_tiles(l, "wo", "m", KD, 2 * l + 1)
                if l == 0:
                    for f in range(F_DENSE):
                        weight_tile((l, "fg", f), "n", KD)
                        weight_tile((l, "fu", f), "n", KD)
                    stream_tiles(l, "dn", "h", F_DENSE, 2 * l + 2)

            l = DEPTH - 1
            for i in range(3):
                lo, n = UT[i]
                out = open_tile((l, "lg", i))
                for k in range(KD):
                    pe.wait_ge(u_ready, KD * (2 * DEPTH - 1) + k + 1)
                    mm = pe.matmul(out[0:n, 0:NEXP], uT[:, k, lo:lo + n], router[:, k, :], start=(k == 0), stop=(k == KD - 1))
                mm.then_inc(mm_done, 1)
            for i in range(6):
                t, half = i // 2, i % 2
                lo, n = UT[t]
                out = open_tile((l, "tt", i))
                for k in range(4):
                    mm = pe.transpose(out[0:n, k * P:(k + 1) * P], uT[:, 4 * half + k, lo:lo + n], ident[:, :])
                mm.then_inc(mm_done, 1)
            pe.wait_ge(route_ready, 1)
            out = open_tile((l, "po", 0))
            for i in range(3):
                n = UT[i][1]
                for x in range(i + 1):
                    k = UT[x][1]
                    left = tri[0:k, 0:n] if x == i else ones[0:k, 0:n]
                    pe.matmul(out[0:n, 8 * i:8 * i + 8], left, rt[0:k, 6, x, :], start=(x == 0), stop=(x == i))
            for x in range(3):
                k = UT[x][1]
                mm = pe.matmul(out[:, 24:32], ones[0:k, :], rt[0:k, 6, x, :], start=(x == 0), stop=(x == 2))
            mm.then_inc(mm_done, 1)

            for i in range(6):
                pe.wait_ge(*out_of((l, "tt", i)))

            def gather():
                for half in range(2):
                    for x in range(4):
                        for i in range(3):
                            n = UT[i][1]
                            c = (4 * half + x) * P
                            mm = pe.matmul(bank[1 + 2 * half][:, x * CAP:(x + 1) * CAP], utok[0:n, i, c:c + P],
                                           sel[0:n, i, :], start=(i == 0), stop=(i == 2))
                    mm.then_inc(misc_done, 1)

            pe.wait_ge(sel_ready, 1)
            for b in (1, 3):
                pe.wait_ge(evicted[b], BASE[b] - 1)
            gather()
            pe.wait_ge(items_ready, 1)
            items = pe.value_load(items_t[0:1, 0:1], min_val=NEXP, max_val=3 * NEXP)
            with pe.Fori(0, items) as it:

                def bank_free(b, use):
                    pe.wait_ge(evicted[b], it * USES[b] + BASE[b] + use)

                def expert_tile(b, t, c):
                    bank_free(b, t // 2)
                    for k in range(KD):
                        if k % 4 == 0:
                            pe.wait_ge(low_done, it * E_CHUNKS + N_CHUNKS + c + k // 4 + 1)
                        w = slice((k % 4) * WIDE, (k % 4 + 1) * WIDE)
                        mm = split_product(bank[b][0:CAP, :], (xg_hi[:, k, :], xg_lo[:, k, :]),
                                           (high_slot(c + k // 4)[:, w], slot(c + k // 4, s5m_parts)[:, w]),
                                           k == 0, k == KD - 1)
                        if k % 4 == 3:
                            mm.then_inc(mm_done, 1)

                def hidden_transpose(t):
                    b = 4 + t % 2
                    bank_free(2 + t % 2, t // 2 + 1)
                    bank_free(b, t // 2)
                    for x in range(4):
                        mm = pe.transpose(bank[b][:, x * CAP:(x + 1) * CAP], hm[0:CAP, t % 2, x * P:(x + 1) * P],
                                          ident[0:CAP, 0:CAP])
                    mm.then_inc(misc_done, 1)

                for b in (1, 3):
                    bank_free(b, 0)
                for t in range(E_TILES):
                    expert_tile(t % 2, t, 4 * t)
                    if t > 0:
                        hidden_transpose(t - 1)
                    expert_tile(2 + t % 2, t, 4 * t + 2)
                for b in (6, 7):
                    bank_free(b, 0)
                for j in range(DN):
                    if j == 2:
                        hidden_transpose(E_TILES - 1)
                        pe.wait_ge(sel_ready, it + 2)
                        bank_free(5, 3)
                        for i in range(3):
                            lo, n = UT[i]
                            mm = pe.transpose(bank[5][0:CAP, lo:lo + n], selw[0:n, i, :], ident[0:n, 0:n])
                        mm.then_inc(misc_done, 1)
                    pe.wait_ge(low_done, it * E_CHUNKS + N_CHUNKS + GU + j + 1)
                    t = j // 2
                    bank_free(4 + t % 2, t // 2 + 1)
                    for x in range(4):
                        f = 2 * j + x // 2
                        w = slice(x * WIDE, (x + 1) * WIDE)
                        mm = split_product(bank[6 + x % 2][0:CAP, :], (hE_hi[:, f, :], hE_lo[:, f, :]),
                                           (high_slot(GU + j)[:, w], slot(GU + j, s5m_parts)[:, w]),
                                           f == 0, f == F_EXP - 1)
                    mm.then_inc(mm_done, 1)
                for b in (1, 3):
                    bank_free(b, 3)
                gather()
                for b in (6, 7):
                    bank_free(b, 1)
                bank_free(5, 4)
                for d in range(KD):
                    b = SCATTER[d % 4]
                    bank_free(b, SCATTER_USE[d % 4] + d // 4)
                    pe.matmul(bank[b][:, 0:T], ytok[0:CAP, d * P:(d + 1) * P], selT[0:CAP, :],
                              start=True, stop=True).then_inc(misc_done, 1)
            pe.wait_ge(evicted[1], items * USES[1] + BASE[1])
            for k in range(KD):
                pe.wait_ge(x_squares, KD * 2 * DEPTH + k + 1)
                mm = pe.matmul(bank[1][:, 0:T], ones[:, :], uT[:, k, :], start=(k == 0), stop=(k == KD - 1))
            mm.then_inc(misc_done, 1)

        @block.scalar
        def _(act):
            split = [0]

            def high_weights(up_to):
                while split[0] <= min(up_to, N_CHUNKS - 1):
                    c = split[0]
                    act.wait_ge(loaded[c % RING], 16 * (c // RING + 1))
                    if c >= HIGHS:
                        act.wait_ge(mm_done, CHUNK_DONE[c - HIGHS])
                    act.activation(weights_hi(c), weights(c, ring), ACT.Copy).then_inc(high_done, 1)
                    split[0] += 1

            def full(key):
                high_weights(CHUNK_OF[key] + 2)
                act.wait_ge(mm_done, DONE[key])

            def evicted_by_dve(key):
                high_weights(CHUNK_OF[key] + 2)
                act.wait_ge(*out_of(key))

            def high(key, whole):
                act.activation(parts(key[1], key[2])[0], whole, ACT.Copy).then_inc(x_high, 1)

            def copy_out(key, dst, src):
                full(key)
                act.activation(dst, src, ACT.Copy).then_inc(freed(key), 1)

            def x_square(d):
                act.activation(uT[:, d, :], xT[:, d, :], ACT.Square).then_inc(x_squares, 1)

            act.wait_ge(ones_set, 2)
            act.wait_ge(lam_in, 16)
            W = lambda i: lw[:, i, :]
            act.activation(W(0), lam[:, 2, :], ACT.Exp).then_inc(lam_act, 1)
            act.wait_ge(x_in, 16)
            for d in range(KD):
                x_square(d)
            act.wait_ge(lam_ready, 1)
            act.activation(W(3), W(1), ACT.Exp).then_inc(lam_act, 1)
            act.activation(W(6), W(4), ACT.Sin).then_inc(lam_act, 1)
            act.activation(W(7), W(5), ACT.Sin).then_inc(lam_act, 1)

            def root(key, scale):
                full(key)
                act.activation(at(key)[:, 0:T], at(key)[:, 0:T], ACT.Sqrt, bias=eps[:, 0:1], scale=scale).then_inc(std_done, 1)

            for l in range(DEPTH):
                root((l, "ms1", 0), 1.0 / D)
                if l == 0:
                    act.wait_ge(consts_in, 16 * 7)
                for d in range(KD):
                    act.wait_ge(u_ready, 2 * KD * l + d + 1)
                    high((l, "u", d), uT[:, d, :])
                for m in range(4):
                    full((l, "cb", m))
                    act.activation(sigb[:, m, :], at((l, "cb", m))[:, 0:T], ACT.Sigmoid, bias=vec(l, V_PWB, 4 + m)
                                   ).then_inc(freed((l, "cb", m)), 1)
                for m in range(4):
                    evicted_by_dve((l, "ca", m))
                for m in range(4):
                    key = (l, "zs", m)
                    full(key)
                    act.activation(sigb[:, m, 0:SEQ].rearrange("p (s c) -> p s c", s=S),
                                   at(key)[:, 0:SEQ].rearrange("p (c s) -> p s c", s=S), ACT.Copy)
                    act.activation(sigb[:, m, SEQ:T], at(key)[:, SEQ:T], ACT.Copy).then_inc(freed(key), 1)
                for m in range(4):
                    evicted_by_dve((l, "zs", m))
                act.dma_start(zscr.rearrange("(m p) t -> p m t", p=P), sigb[:, :, :]).then_inc(zscr_out, 16)
                for m in range(KD):
                    copy_out((l, "v", m), vT[:, m, :], at((l, "v", m))[:, 0:T])
                    if m == 2:
                        act.wait_ge(xin_zero, 1)
                        act.wait_ge(zscr_out, 16 * (l + 1))
                        zg = zscr.rearrange("(g p) t -> p g t", p=GP)
                        for s in range(S):
                            act.dma_start(xin[s * GP:(s + 1) * GP, :, 0:NC], zg[:, :, s * NC:(s + 1) * NC]).then_inc(xin_in, 16)
                        act.dma_start(xin[0:GP, :, NC:NC + NS], zg[:, :, SEQ:T]).then_inc(xin_in, 16)
                        act.dma_start(xin[P - GP:P, :, NC + NS:NC + 2 * NS], zg[:, :, SEQ:T]).then_inc(xin_in, 16)
                act.wait_ge(gb_ready, l + 1)
                for i in range(4):
                    copy_out((l, "vt", i), vtok[:, i // 2, (i % 2) * 512:(i % 2 + 1) * 512], at((l, "vt", i))[:, :])
                for i in range(2):
                    copy_out((l, "vs", i), vst[0:NS, i * 512:(i + 1) * 512], at((l, "vs", i))[0:NS, :])
                copy_out((l, "ks", 0), kst[0:NS, :], at((l, "ks", 0))[0:NS, :])
                for i in range(8):
                    copy_out((l, "win", i), winT[:, i * 512:(i + 1) * 512], at((l, "win", i))[:, :])
                for i in range(8):
                    copy_out((l, "kk", i), s5m[0:GP, i * 512:(i + 1) * 512], at((l, "kk", i))[0:GP, :])
                for h in range(HEADS):
                    key = (l, "ou", h)
                    full(key)
                    act.activation(vT[:, 2 * h:2 * h + 2, 0:SEQ], at(key)[:, :].rearrange("p (x t) -> p x t", x=2),
                                   ACT.Copy).then_inc(freed(key), 1)
                    key = (l, "st", h)
                    copy_out(key, stst[:, h, :], at(key)[:, 0:DV])
                for i in range(4):
                    key = (l, "si", i)
                    copy_out(key, si[:, :, 4 * i:4 * i + 4, :].rearrange("p r j c -> p j r c"),
                             at(key)[:, 0:384].rearrange("p (j r c) -> p j r c", j=4, r=2))
                evicted_by_dve((l, "cm", 0))
                act.wait_ge(st_out, 16 * (l + 1))
                act.activation(sq[:, :].rearrange("p (m t) -> p m t", m=4), cT[:, :, :], ACT.Square).then_inc(squares, 1)
                root((l, "cv", 0), 1.0 / 512)
                act.wait_ge(cn_ready, l + 1)
                for m in range(4):
                    act.activation(cT[:, m, :], cT[:, m, :], ACT.Silu, bias=vec(l, V_LNB, m), scale=vec(l, V_LNG, m)
                                   ).then_inc(c_act, 1)
                for m in range(4):
                    act.wait_ge(c_act, 4 * l + m + 1)
                    high((l, "c", m), cT[:, m, :])

                def sample_out(b):
                    key = (l, "os", b)
                    copy_out(key, vT[:, :, SEQ + b:SEQ + b + 1], at(key)[:, 0:KD].rearrange("p (m o) -> p m o", o=1))

                for d in range(KD):
                    key = (l, "gc", d)
                    full(key)
                    if d >= 2:
                        evicted_by_dve((l, "pc", d - 2))
                    act.activation(gate[:, d % 2, :], at(key)[:, 0:T], ACT.Sigmoid).then_inc(freed(key), 1)
                    if d > 0:
                        sample_out(d - 1)
                sample_out(NS - 1)
                for h in range(HEADS):
                    evicted_by_dve((l, "gm", h))
                    if h >= 2:
                        full((l, "gv", h - 2))
                    c = (h % 2) * 2 * T
                    act.activation(sq[:, c:c + 2 * T].rearrange("p (x t) -> p x t", x=2), vT[:, 2 * h:2 * h + 2, :],
                                   ACT.Square).then_inc(squares, 1)
                    if h >= 1:
                        root((l, "gv", h - 1), 1.0 / DV)
                root((l, "gv", 3), 1.0 / DV)
                for i in range(8):
                    copy_out((l, "y", i), yst[0:NC + NS, :, 4 * i:4 * i + 4, :].rearrange("c s g q -> c g s q"),
                             at((l, "y", i))[0:NC + NS, :].rearrange("c (g s q) -> c g s q", g=4, s=S))
                for m in range(KD):
                    key = (l, "gg", m)
                    full(key)
                    if m >= 2:
                        act.wait_ge(gated, KD * l + m - 1)
                    else:
                        evicted_by_dve((l, "pc", 6 + m))
                    act.activation(gate[:, m % 2, :], at(key)[:, 0:T], ACT.Silu).then_inc(freed(key), 1)
                    if m >= 2:
                        high((l, "r", m - 2), vT[:, m - 2, :])
                for m in (KD - 2, KD - 1):
                    act.wait_ge(gated, KD * l + m + 1)
                    high((l, "r", m), vT[:, m, :])
                act.wait_ge(conv_state_out, 32 * (l + 1))
                for m in range(4):
                    key = (l, "yt", m)
                    full(key)
                    first, rest = at(key)[:, 0:NC], at(key)[:, NC + NS:T].rearrange("p (s c) -> p c s", s=S - 1)
                    to = yg[:, m, 0:SEQ].rearrange("p (c s) -> p c s", s=S)
                    act.activation(to[:, :, 0], first, ACT.Gelu_apprx_tanh).then_inc(gelu_done, 1)
                    act.activation(to[:, :, 1:S], rest, ACT.Gelu_apprx_tanh).then_inc(gelu_done, 1)
                    act.activation(yg[:, m, SEQ:T], at(key)[:, NC:NC + NS], ACT.Gelu_apprx_tanh).then_inc(freed(key), 1)
                for d in range(KD):
                    key = (l, "gr", d)
                    full(key)
                    if d >= 2:
                        evicted_by_dve((l, "pr", d - 2))
                    else:
                        act.wait_ge(gated, KD * l + 7 + d)
                    act.activation(gate[:, d % 2, :], at(key)[:, 0:T], ACT.Sigmoid).then_inc(freed(key), 1)
                    if d == 2:
                        act.wait_ge(gelu_done, 8 * (l + 1))
                        for m in range(4):
                            act.wait_ge(*out_of((l, "yt", m)))
                            high((l, "y", m), yg[:, m, :])
                for m in range(4):
                    key = (l, "gl", m)
                    full(key)
                    if m >= 2:
                        act.wait_ge(glu_done, 4 * l + m - 1)
                    else:
                        evicted_by_dve((l, "pr", 6 + m))
                    act.activation(gate[:, m % 2, :], at(key)[:, 0:T], ACT.Sigmoid, bias=vec(l, V_GLB, m)).then_inc(freed(key), 1)
                    if m >= 2:
                        high((l, "g", m - 2), sigb[:, m - 2, :])
                for m in (2, 3):
                    act.wait_ge(glu_done, 4 * l + m + 1)
                    high((l, "g", m), sigb[:, m, :])
                for d in range(KD):
                    key = (l, "gs", d)
                    full(key)
                    if d >= 2:
                        evicted_by_dve((l, "ps", d - 2))
                    act.activation(gate[:, d % 2, :], at(key)[:, 0:T], ACT.Sigmoid).then_inc(freed(key), 1)
                    if d >= 2:
                        act.wait_ge(merged, 16 * l + KD + d - 1)
                        high((l, "m", d - 2), mT[:, d - 2, :])
                for d in (KD - 2, KD - 1):
                    high_weights(CHUNK_OF[(l, "ps", d)] + 2)
                    act.wait_ge(merged, 16 * l + KD + d + 1)
                    high((l, "m", d), mT[:, d, :])
                for d in range(KD):
                    evicted_by_dve((l, "wo", d))
                    x_square(d)
                root((l, "ms2", 0), 1.0 / D)
                if l == 0:
                    for d in range(KD):
                        act.wait_ge(u_ready, KD * (2 * l + 1) + d + 1)
                        high((l, "n", d), uT[:, d, :])
                    for f in range(F_DENSE):
                        key = (l, "fg", f)
                        full(key)
                        if f >= 2:
                            evicted_by_dve((l, "fu", f - 2))
                        else:
                            evicted_by_dve((l, "ps", 6 + f))
                        act.activation(gate[:, f % 2, :], at(key)[:, 0:T], ACT.Silu).then_inc(freed(key), 1)
                        if f >= 2:
                            high((l, "h", f - 2), hT[:, f - 2, :])
                    for f in (F_DENSE - 2, F_DENSE - 1):
                        evicted_by_dve((l, "fu", f))
                        high((l, "h", f), hT[:, f, :])
                    for d in range(KD):
                        evicted_by_dve((l, "dn", d))
                        x_square(d)

            l = DEPTH - 1
            act.wait_ge(s_out[0], 64 * DEPTH)
            act.wait_ge(s_out[1], 64 * DEPTH)
            act.wait_ge(st_out, 16 * DEPTH)
            act.wait_ge(hstate_out, 32 * DEPTH)
            for i in range(6):
                n = UT[i // 2][1]
                copy_out((l, "tt", i), utok[0:n, i // 2, (i % 2) * 512:(i % 2 + 1) * 512], at((l, "tt", i))[0:n, :])
            act.wait_ge(route_act, 1)
            act.activation(rt[:, 2, :, 0:1], rt[:, 1, :, 0:1], ACT.Exp).then_inc(route_act, 1)
            act.wait_ge(items_ready, 1)
            items = act.value_load(items_t[0:1, 0:1], min_val=NEXP, max_val=3 * NEXP)

            def gathered(turn):
                for half in range(2):
                    act.wait_ge(misc_done, turn + half)
                    act.activation(xg_hi[:, 4 * half:4 * half + 4, :],
                                   bank[1 + 2 * half][:, 0:4 * CAP].rearrange("p (k c) -> p k c", k=4), ACT.Copy
                                   ).then_inc(gathered_high, 1)

            def high_experts(it, c):
                act.wait_ge(mloaded[c % MRING], (it * TURNS + c // MRING + 1) * 16)
                act.wait_ge(mm_done, it * E_CHUNKS + MM_BASE + c - HRING + 1)
                act.activation(high_slot(c), slot(c, s5m), ACT.Copy).then_inc(high_done, 1)

            for c in range(AHEAD):
                high_experts(0, c)
            gathered(1)
            with act.Fori(0, items) as it:
                for c in range(E_CHUNKS):
                    t = c // 4
                    if c < GU and c % 4 == 1:
                        act.wait_ge(mm_done, it * E_CHUNKS + MM_BASE + c + 1)
                        act.activation(hm[0:CAP, t % 2, :], bank[t % 2][0:CAP, :], ACT.Silu).then_inc(evicted[t % 2], 1)
                    if c == GU + 2 or (c < GU and c % 4 == 2 and c > 4):
                        act.wait_ge(misc_done, it * MISC + MISC0 + t)
                        act.activation(hE_hi[:, 4 * t - 4:4 * t, :],
                                       bank[4 + (t - 1) % 2][:, 0:4 * CAP].rearrange("p (k c) -> p k c", k=4), ACT.Copy
                                       ).then_inc(hidden_high, 1)
                    if c == GU + 2:
                        act.wait_ge(misc_done, it * MISC + MISC0 + M_ONEHOT + 1)
                        act.activation(selT[0:CAP, :], bank[5][0:CAP, 0:T], ACT.Copy).then_inc(evicted[5], 1)
                    if c < E_CHUNKS - 1:
                        high_experts(it, c + AHEAD)
                act.wait_ge(mm_done, it * E_CHUNKS + MM_BASE + E_CHUNKS)
                act.activation(ytok[0:CAP, 0:WIDE], bank[6][0:CAP, :], ACT.Copy).then_inc(evicted[6], 1)
                gathered(it * MISC + MISC0 + M_GATHER + 1)
                high_experts(it, E_CHUNKS - 1 + AHEAD)
            for d in range(KD):
                b = SCATTER[d % 4]
                act.wait_ge(evicted[b], items * USES[b] + BASE[b] - (d < 4))
                x_square(d)
            act.wait_ge(misc_done, items * MISC + MISC0 + 1)
            act.activation(bank[1][:, 0:T], bank[1][:, 0:T], ACT.Sqrt, bias=eps[:, 0:1], scale=1.0 / D).then_inc(std_done, 1)

        @block.vector
        def _(dve):
            order = [0]

            def link(ins):
                order[0] += 1
                ins.then_inc(dve_order, 1)
                dve.wait_ge(dve_order, order[0])

            split = [0]

            def low_weights(up_to):
                while split[0] <= min(up_to, N_CHUNKS - 1):
                    c = split[0]
                    dve.wait_ge(high_done, c + 1)
                    dve.tensor_tensor(weights(c, ring_parts), weights(c, ring), f32(weights_hi(c)), ALU.subtract
                                      ).then_inc(low_done, 1)
                    split[0] += 1

            def full(key):
                low_weights(CHUNK_OF[key] + 2)
                dve.wait_ge(mm_done, DONE[key])

            def evicted_by_act(key):
                low_weights(CHUNK_OF[key] + 2)
                dve.wait_ge(*out_of(key))

            def low(key, whole):
                dve.wait_ge(x_high, PART[key])
                high, to = parts(key[1], key[2])
                dve.tensor_tensor(to, whole, f32(high), ALU.subtract).then_inc(x_low, 1)

            def mul(out, x, y):
                return dve.tensor_tensor(out, x, y, ALU.mult)

            def add(out, x, y):
                return dve.tensor_tensor(out, x, y, ALU.add)

            dve.memset(ones[:, :], 1.0).then_inc(ones_set, 1)
            dve.memset(eps[:, :], EPS).then_inc(ones_set, 1)
            W = lambda i: lw[:, i, :]
            lre, lim = lam[:, 0, :], lam[:, 1, :]
            TWO_PI_HI = 6.28125
            TWO_PI_LO = 2 * np.pi - 6.28125
            ROUND = 1.5 * 2 ** 23
            HALF_PI = np.pi / 2
            PI_DOWN = 3.1415925
            dve.wait_ge(lam_in, 16)
            dve.wait_ge(lam_act, 1)
            link(mul(W(1), lre, W(0)))
            link(mul(W(2), lim, W(0)))
            link(dve.tensor_scalar(W(14), W(2), 1 / (2 * np.pi), None, ALU.mult))
            link(dve.tensor_scalar(W(14), W(14), ROUND, None, ALU.add))
            link(dve.tensor_scalar(W(14), W(14), -ROUND, None, ALU.add))
            link(dve.scalar_tensor_tensor(out=W(4), in0=W(14), scalar=-TWO_PI_HI, in1=W(2), op0=ALU.mult, op1=ALU.add))
            link(dve.scalar_tensor_tensor(out=W(4), in0=W(14), scalar=-TWO_PI_LO, in1=W(4), op0=ALU.mult, op1=ALU.add))
            link(dve.tensor_scalar(W(4), W(4), PI_DOWN, -PI_DOWN, ALU.min, ALU.max))
            link(dve.tensor_scalar(W(15), W(4), -1.0, None, ALU.mult))
            link(dve.tensor_tensor(W(15), W(15), W(4), ALU.max))
            dve.tensor_scalar(W(5), W(15), -1.0, HALF_PI, ALU.mult, ALU.add).then_inc(lam_ready, 1)
            link(mul(W(10), lre, lre))
            link(mul(W(14), lim, lim))
            link(add(W(10), W(10), W(14)))
            link(dve.reciprocal(W(10), W(10)))
            dve.wait_ge(lam_act, 4)
            link(mul(W(8), W(3), W(7)))
            link(mul(W(9), W(3), W(6)))
            link(dve.tensor_scalar(W(11), W(8), -1.0, None, ALU.add))
            link(mul(W(12), W(11), lre))
            link(mul(W(14), W(9), lim))
            link(add(W(12), W(12), W(14)))
            link(mul(W(12), W(12), W(10)))
            link(mul(W(13), W(9), lre))
            link(mul(W(14), W(11), lim))
            link(dve.tensor_tensor(W(13), W(13), W(14), ALU.subtract))
            mul(W(13), W(13), W(10)).then_inc(lam_ready, 1)
            dve.wait_ge(x_in, 16)
            dve.wait_ge(consts_in, 16 * 7)

            def normed(key, gains, turn, part):
                low_weights(CHUNK_OF[key] + 2)
                dve.wait_ge(std_done, turn)
                dve.reciprocal(rstd[:, 0, :], at(key)[:, 0:T]).then_inc(freed(key), 1)
                dve.wait_ge(*out_of(key))
                for d in range(KD + 2):
                    if d < KD:
                        dve.scalar_tensor_tensor(out=uT[:, d, :], in0=xT[:, d, :], scalar=gains(d), in1=rstd[:, 0, :],
                                                 op0=ALU.mult, op1=ALU.mult).then_inc(u_ready, 1)
                    if part and d >= 2:
                        low((key[0], part, d - 2), uT[:, d - 2, :])

            def conv_ops(l, lo, hi):
                for n in range(lo, hi):
                    k, m = n // 4, n % 4
                    if k == 0:
                        evicted_by_act((l, "ca", m))
                        dve.tensor_scalar(cT[:, m, 0:SEQ], xc[:, m, 0:SEQ], vec(l, V_DWW, m * TAPS), vec(l, V_DWB, m),
                                          ALU.mult, ALU.add).then_inc(conv_step, 1)
                    else:
                        dve.wait_ge(conv_step, l * 4 * TAPS + n - 3)
                        dve.scalar_tensor_tensor(out=cT[:, m, 0:SEQ], in0=xc[:, m, k:k + SEQ],
                                                 scalar=vec(l, V_DWW, m * TAPS + k), in1=cT[:, m, 0:SEQ],
                                                 op0=ALU.mult, op1=ALU.add).then_inc(conv_step, 1)

            def recur(l, lo, hi):
                for c in range(lo, hi):
                    to = c + 1 if c + 1 < NC else NC + NS
                    now = hst[:, :, :, c]
                    mul(rec[:, 0, :, :], now, l8[:, 0:2, :]).then_inc(dve_order, 1)
                    mul(rec[:, 1, 0, :], hst[:, 1, :, c], l8[:, 2, :]).then_inc(dve_order, 1)
                    mul(rec[:, 1, 1, :], hst[:, 0, :, c], l8[:, 3, :]).then_inc(dve_order, 1)
                    order[0] += 3
                    dve.wait_ge(dve_order, order[0] - 2)
                    link(add(rec[:, 2, :, :], rec[:, 0, :, :], si[:, :, :, c]))
                    link(add(hst[:, :, :, to], rec[:, 1, :, :], rec[:, 2, :, :]))

            for l in range(DEPTH):
                normed((l, "ms1", 0), lambda d: vec(l, V_GM, d), 7 * l + 1, "u")
                link(dve.memset(xc[:, :, 0:TAPS - 1], 0.0))
                for m in range(4):
                    key = (l, "ca", m)
                    evicted_by_act((l, "cb", m))
                    full(key)
                    dve.scalar_tensor_tensor(out=xc[:, m, TAPS - 1:TAPS - 1 + SEQ], in0=at(key)[:, 0:SEQ],
                                             scalar=vec(l, V_PWB, m), in1=sigb[:, m, 0:SEQ], op0=ALU.add, op1=ALU.mult)
                    dve.scalar_tensor_tensor(out=xs[:, m, :, TAPS - 1], in0=at(key)[:, SEQ:T],
                                             scalar=vec(l, V_PWB, m), in1=sigb[:, m, SEQ:T], op0=ALU.add, op1=ALU.mult
                                             ).then_inc(freed(key), 1)
                for m in range(4):
                    low_weights(CHUNK_OF[(l, "zs", m)] + 2)
                    conv_ops(l, 4 * m, 4 * m + 4)
                dve.wait_ge(table_in, 16 * (2 * l + 1))
                for n in range(8):
                    name, h = ("q", n) if n < 4 else ("k", n - 4)
                    to = qT if n < 4 else kT
                    w = 0 if n < 4 else 2
                    key = (l, name, h)
                    full(key)
                    if n > 0:
                        prev = (l, "q", n - 1) if n <= 4 else (l, "k", n - 5)
                        evicted_by_act(prev)
                    s = 1.0 if n < 4 else P ** -0.5

                    def turned(out, x, y):
                        return dve.scalar_tensor_tensor(out=out, in0=x, scalar=s, in1=y, op0=ALU.mult, op1=ALU.mult)

                    turned(tmp[:, 0, :], at(key)[:, 0:T], rope[:, 0, :])
                    turned(tmp[0:64, 1, :], at(key)[64:P, 0:T], rope[64:P, 1, :])
                    link(turned(tmp[64:P, 1, :], at(key)[0:64, 0:T], rope[0:64, 1, :]))
                    add(to[:, h, :], tmp[:, 0, :], tmp[:, 1, :]).then_inc(freed(key), 1)
                dve.wait_ge(*out_of((l, "q", 3)))
                dve.tensor_copy(qs[:, :, :], qT[:, :, SEQ:T]).then_inc(qs_ready, 1)
                for m in range(8):
                    low_weights(CHUNK_OF[(l, "v", m)] + 2)
                    conv_ops(l, 16 + 4 * m, 20 + 4 * m)
                dve.wait_ge(gb_ready, l + 1)
                for i in range(2):
                    key = (l, "kt", i)
                    full(key)
                    dve.tensor_tensor(kd[:, i, :].rearrange("p (h x) -> p h x", h=HEADS),
                                      at(key)[:, :].rearrange("p (h x) -> p h x", h=HEADS),
                                      kdec[:, i, :].unsqueeze(2).broadcast_to([P, HEADS, P]), ALU.mult).then_inc(freed(key), 1)
                conv_ops(l, 48, 92)
                dve.wait_ge(table_in, 16 * (2 * l + 2))
                for h in range(HEADS):
                    key = (l, "sc", h)
                    full(key)
                    mul(pt[:, h % 2, 0:SEQ], at(key)[:, 0:SEQ], decay[:, h, :])
                    mul(pt[:, h % 2, SEQ:SEQ + P], at(key)[:, SEQ:SEQ + P], decay[:, h, 0:P]).then_inc(freed(key), 1)
                    conv_ops(l, 92 + 8 * h, 100 + 8 * h)
                dve.wait_ge(conv_state_in, 16 * (l + 1))
                evicted_by_act((l, "k", 3))
                prod = tmp[:, :, :].rearrange("p a t -> p (a t)")[:, 0:NS * TAPS].rearrange("p (b k) -> p b k", b=NS)
                for m in range(4):
                    taps = vecs[:, l * V_L + V_DWW + m * TAPS:l * V_L + V_DWW + (m + 1) * TAPS]
                    link(mul(prod, xs[:, m, :, :], taps.unsqueeze(1).broadcast_to([P, NS, TAPS])))
                    link(dve.tensor_reduce(cT[:, m, SEQ:T], prod, AX, ALU.add))
                    if m < 3:
                        link(dve.tensor_scalar(cT[:, m, SEQ:T], cT[:, m, SEQ:T], vec(l, V_DWB, m), None, ALU.add))
                dve.wait_ge(conv_step, (l + 1) * 4 * TAPS)
                dve.tensor_scalar(cT[:, 3, SEQ:T], cT[:, 3, SEQ:T], vec(l, V_DWB, 3), None, ALU.add).then_inc(conv_done, 1)
                key = (l, "cm", 0)
                full(key)
                dve.scalar_tensor_tensor(out=cT[:, :, :], in0=at(key)[:, 0:T].unsqueeze(1).broadcast_to([P, 4, T]),
                                         scalar=-1.0 / 512, in1=cT[:, :, :], op0=ALU.mult, op1=ALU.add).then_inc(freed(key), 1)

                def kmasked(b):
                    if b >= 2:
                        full((l, "ob", b - 2))
                    dve.tensor_scalar(kmask[0:NS, b % 2, :], kst[0:NS, :], ident[0:NS, b:b + 1], None, ALU.mult
                                      ).then_inc(kmask_ready, 1)

                evicted_by_act((l, "ks", 0))
                kmasked(0)
                kmasked(1)
                key = (l, "cv", 0)
                dve.wait_ge(std_done, 7 * l + 2)
                dve.reciprocal(rstd[:, 0, :], at(key)[:, 0:T]).then_inc(freed(key), 1)
                evicted_by_act(key)
                mul(cT[:, :, :], cT[:, :, :], rstd[:, 0, :].unsqueeze(1).broadcast_to([P, 4, T])).then_inc(cn_ready, 1)
                for m in range(4):
                    low((l, "c", m), cT[:, m, :])
                for i in range(4):
                    evicted_by_act((l, "si", i))
                dve.wait_ge(l8_ready, l + 1)
                dve.wait_ge(h0_in, 16 * (l + 1))
                link(dve.memset(hst[:, :, :, 0:1], 0.0))
                for d in range(KD):
                    recur(l, 4 * d, 4 * d + 4)
                    key = (l, "pc", d)
                    evicted_by_act((l, "gc", d))
                    full(key)
                    mul(mT[:, d, :], at(key)[:, 0:T], gate[:, d % 2, :]).then_inc(freed(key), 1)
                    dve.wait_ge(s_in[d % 2], 16 * (4 * l + d // 2 + 1))
                    for half, name in ((0, "oa"), (1, "ob")):
                        key = (l, name, d)
                        full(key)
                        for x in range(2):
                            h = 2 * half + x
                            s = sring[:, d % 2, h, :]
                            last = dve.scalar_tensor_tensor(out=s, in0=s, scalar=1.0 - 2.0 ** (-5 - h),
                                                            in1=at(key)[:, x * DV:(x + 1) * DV], op0=ALU.mult, op1=ALU.add)
                        last.then_inc(freed(key), 1)
                    if d + 2 < NS:
                        kmasked(d + 2)
                if l > 0:
                    dve.wait_ge(hstate_out, 32 * l)
                link(dve.tensor_copy(hfin[:, :, :], hst[:, :, :, NC + NS]))
                h0 = hst[:, :, :, NC:NC + NS]
                lb = [lw[:, w, l * GJ:(l + 1) * GJ] for w in (8, 9)]
                t = tmp[:, 0, 0:GJ * NS].rearrange("p (j b) -> p j b", j=GJ)
                wide = [P, GJ, NS]
                for ri in range(2):
                    link(mul(hnew[:, ri, :, :], h0[:, ri, :, :], lb[0].unsqueeze(2).broadcast_to(wide)))
                    link(mul(t, h0[:, 1 - ri, :, :], lb[1].unsqueeze(2).broadcast_to(wide)))
                    link(dve.tensor_tensor(hnew[:, ri, :, :], hnew[:, ri, :, :], t, ALU.add if ri else ALU.subtract))
                add(hnew[:, :, :, :], hnew[:, :, :, :], si[:, :, :, NC + NS:NC + 2 * NS]).then_inc(h_ready, 1)
                for h in range(HEADS):
                    key = (l, "gm", h)
                    full(key)
                    dve.scalar_tensor_tensor(out=vT[:, 2 * h:2 * h + 2, :],
                                             in0=at(key)[:, 0:T].unsqueeze(1).broadcast_to([P, 2, T]), scalar=-1.0 / DV,
                                             in1=vT[:, 2 * h:2 * h + 2, :], op0=ALU.mult, op1=ALU.add).then_inc(freed(key), 1)
                for h in range(HEADS):
                    key = (l, "gv", h)
                    dve.wait_ge(std_done, 7 * l + 3 + h)
                    dve.reciprocal(rstd[:, h % 2, :], at(key)[:, 0:T]).then_inc(freed(key), 1)
                    evicted_by_act(key)
                    link(mul(vT[:, 2 * h:2 * h + 2, :], vT[:, 2 * h:2 * h + 2, :],
                             rstd[:, h % 2, :].unsqueeze(1).broadcast_to([P, 2, T])))
                for m in range(KD):
                    evicted_by_act((l, "gg", m))
                    mul(vT[:, m, :], vT[:, m, :], gate[:, m % 2, :]).then_inc(gated, 1)
                    if m >= 3:
                        low((l, "r", m - 3), vT[:, m - 3, :])
                for m in range(KD - 3, KD):
                    low((l, "r", m), vT[:, m, :])

                def merge(gate_name, proj_name, turn):
                    for d in range(KD):
                        key = (l, proj_name, d)
                        evicted_by_act((l, gate_name, d))
                        full(key)
                        mul(tmp[:, d % 2, :], at(key)[:, 0:T], gate[:, d % 2, :]).then_inc(freed(key), 1)
                        evicted_by_act(key)
                        if turn == 0:
                            evicted_by_act((l, "pc", d))
                        else:
                            dve.wait_ge(merged, 16 * l + d + 1)
                        add(mT[:, d, :], mT[:, d, :], tmp[:, d % 2, :]).then_inc(merged, 1)
                        if turn == 0 and d == 3:
                            for m in range(4):
                                low((l, "y", m), yg[:, m, :])
                        if turn == 1 and d >= 2:
                            low((l, "m", d - 2), mT[:, d - 2, :])

                merge("gr", "pr", 0)
                for m in range(4):
                    evicted_by_act((l, "gl", m))
                    mul(sigb[:, m, :], yg[:, m, :], gate[:, m % 2, :]).then_inc(glu_done, 1)
                    if m >= 2:
                        low((l, "g", m - 2), sigb[:, m - 2, :])
                for m in (2, 3):
                    low((l, "g", m), sigb[:, m, :])
                merge("gs", "ps", 1)
                for d in (KD - 2, KD - 1):
                    low((l, "m", d), mT[:, d, :])
                for d in range(KD):
                    key = (l, "wo", d)
                    full(key)
                    add(xT[:, d, :], xT[:, d, :], at(key)[:, 0:T]).then_inc(freed(key), 1)
                normed((l, "ms2", 0), lambda d: vec(l, V_GF, d), 7 * l + 7, "n" if l == 0 else None)
                if l == 0:
                    for f in range(F_DENSE):
                        key = (l, "fu", f)
                        evicted_by_act((l, "fg", f))
                        full(key)
                        mul(hT[:, f, :], at(key)[:, 0:T], gate[:, f % 2, :]).then_inc(freed(key), 1)
                        if f >= 3:
                            low((l, "h", f - 3), hT[:, f - 3, :])
                    for f in range(F_DENSE - 3, F_DENSE):
                        low((l, "h", f), hT[:, f, :])
                    for d in range(KD):
                        key = (l, "dn", d)
                        full(key)
                        add(xT[:, d, :], xT[:, d, :], at(key)[:, 0:T]).then_inc(freed(key), 1)

            l = DEPTH - 1
            R = lambda w: rt[:, w, :, :]
            R1 = lambda w, c=0: rt[:, w, :, c:c + 1]
            for b in range(2):
                dve.wait_ge(s_out[b], 64 * DEPTH)
            dve.wait_ge(st_out, 16 * DEPTH)
            dve.wait_ge(hstate_out, 32 * DEPTH)
            link(dve.memset(rt[:, :, :, :], 0.0))
            link(dve.memset(slotx[:, :, :], -BIG))
            link(dve.memset(combx[:, :, :], 0.0))
            for i in range(3):
                key = (l, "lg", i)
                full(key)
                n = UT[i][1]
                dve.tensor_copy(rt[0:n, 0, i, :], at(key)[0:n, 0:NEXP]).then_inc(freed(key), 1)
            for i in range(3):
                evicted_by_act((l, "lg", i))
                link(dve.max(rt[:, 8, i, :], rt[:, 0, i, :]))
                link(dve.max_index(rti[:, i, :], rt[:, 8, i, :], rt[:, 0, i, :]))
            link(dve.tensor_copy(R(9), rti[:, :, :]))
            wide = [P, 3, NEXP]
            eight = iota[:, 0:NEXP].unsqueeze(1).broadcast_to(wide)
            dve.tensor_tensor(R1(1), R1(8, 1), R1(8, 0), ALU.subtract).then_inc(route_act, 1)
            link(dve.tensor_tensor(R(10), eight, R1(9, 0).broadcast_to(wide), ALU.is_equal))
            link(dve.tensor_tensor(R(11), eight, R1(9, 1).broadcast_to(wide), ALU.is_equal))
            add(R(6), R(10), R(11)).then_inc(route_ready, 1)
            dve.wait_ge(route_act, 2)
            link(dve.tensor_scalar(R1(3), R1(2), 1.0, None, ALU.add))
            link(dve.reciprocal(R1(4), R1(3)))
            link(mul(R1(5), R1(2), R1(4)))
            link(mul(R(13), R(10), R1(4).broadcast_to(wide)))
            link(mul(R(14), R(11), R1(5).broadcast_to(wide)))
            link(add(R(7), R(13), R(14)))
            dve.wait_ge(route_ready, 1)
            link(dve.tensor_scalar(R(15), R(6), BIG, -BIG, ALU.mult, ALU.add))
            key = (l, "po", 0)
            full(key)
            o = at(key)
            link(add(rt[:, 12, 0:2, :], rt[:, 15, 0:2, :], o[:, 0:16].rearrange("p (i e) -> p i e", i=2)))
            link(add(rt[0:NS, 12, 2, :], rt[0:NS, 15, 2, :], o[0:NS, 16:24]))
            for i in range(3):
                last = dve.tensor_scalar(sel[:, i, :], iota[:, :], rt[:, 12, i, 0:1], None, ALU.is_equal)
            last.then_inc(sel_ready, 1)
            dve.tensor_reduce(rt[:, 16, 0, 0:1], o[:, 24:32], AX, ALU.max).then_inc(freed(key), 1)
            evicted_by_act(key)
            link(dve.tensor_scalar(rt[:, 16, 0, 1:2], rt[:, 16, 0, 0:1], float(CAP), None, ALU.is_gt))
            link(dve.tensor_scalar(rt[:, 16, 0, 2:3], rt[:, 16, 0, 0:1], float(2 * CAP), None, ALU.is_gt))
            link(add(rt[:, 16, 0, 3:4], rt[:, 16, 0, 1:2], rt[:, 16, 0, 2:3]))
            dve.tensor_scalar(items_t[:, :], rt[:, 16, 0, 3:4], float(NEXP), float(NEXP), ALU.mult, ALU.add
                              ).then_inc(items_ready, 1)
            for r in range(3):
                c = slice(r * NEXP, (r + 1) * NEXP)
                link(dve.tensor_scalar(slotx[:, :, c], R(12), -float(CAP * r), None, ALU.add))
                link(dve.tensor_copy(combx[:, :, c], R(7)))
            dve.wait_ge(items_ready, 1)
            items = dve.value_load(items_t[0:1, 0:1], min_val=NEXP, max_val=3 * NEXP)
            def gathered(turn):
                for half in range(2):
                    dve.wait_ge(gathered_high, turn + half)
                    x = xg_hi[:, 4 * half:4 * half + 4, :]
                    dve.tensor_tensor(xg_lo[:, 4 * half:4 * half + 4, :],
                                      bank[1 + 2 * half][:, 0:4 * CAP].rearrange("p (k c) -> p k c", k=4), f32(x), ALU.subtract
                                      ).then_inc(evicted[1 + 2 * half], 1)

            def low_experts(it, c):
                dve.wait_ge(high_done, it * E_CHUNKS + N_CHUNKS + c + 1)
                dve.tensor_tensor(slot(c, s5m_parts), slot(c, s5m), f32(high_slot(c)), ALU.subtract).then_inc(low_done, 1)

            for c in range(AHEAD):
                low_experts(0, c)
            gathered(1)
            with dve.Fori(0, items) as it:
                for c in range(E_CHUNKS):
                    t = c // 4
                    if c < GU and c % 4 == 3:
                        dve.wait_ge(mm_done, it * E_CHUNKS + MM_BASE + c + 1)
                        dve.wait_ge(evicted[t % 2], it * USES[t % 2] + BASE[t % 2] + t // 2 + 1)
                        mul(hm[0:CAP, t % 2, :], hm[0:CAP, t % 2, :], bank[2 + t % 2][0:CAP, :]).then_inc(evicted[2 + t % 2], 1)
                    if c == GU + 2 or (c < GU and c % 4 == 2 and c > 4):
                        b = 4 + (t - 1) % 2
                        dve.wait_ge(hidden_high, it * E_TILES + t)
                        dve.tensor_tensor(hE_lo[:, 4 * t - 4:4 * t, :], bank[b][:, 0:4 * CAP].rearrange("p (k c) -> p k c", k=4),
                                          f32(hE_hi[:, 4 * t - 4:4 * t, :]), ALU.subtract).then_inc(evicted[b], 1)
                    if c == 9:
                        dve.wait_ge(misc_done, it * MISC + MISC0)
                        dve.tensor_copy(cur[:, 0, :], slotx[:, :, bass.ds(it + 1, 1)].rearrange("p i o -> p (i o)")).then_inc(cur_ready, 1)
                        dve.tensor_copy(cur[:, 1, :], slotx[:, :, bass.ds(it, 1)].rearrange("p i o -> p (i o)")).then_inc(cur_ready, 1)
                        dve.tensor_copy(cur[:, 2, :], combx[:, :, bass.ds(it, 1)].rearrange("p i o -> p (i o)")).then_inc(cur_ready, 1)
                        dve.wait_ge(cur_ready, it * 3 + 3)
                        for i in range(3):
                            dve.tensor_scalar(sel[:, i, :], iota[:, :], cur[:, 0, i:i + 1], None, ALU.is_equal)
                            last = dve.tensor_scalar(selw[:, i, :], iota[:, :], cur[:, 1, i:i + 1], cur[:, 2, i:i + 1],
                                                     ALU.is_equal, ALU.mult)
                        last.then_inc(sel_ready, 1)
                    if c < E_CHUNKS - 1:
                        low_experts(it, c + AHEAD)
                dve.wait_ge(mm_done, it * E_CHUNKS + MM_BASE + E_CHUNKS)
                dve.tensor_copy(ytok[0:CAP, WIDE:D], bank[7][0:CAP, :]).then_inc(evicted[7], 1)
                gathered(it * 2 + 3)
                for d in range(KD):
                    b = SCATTER[d % 4]
                    dve.wait_ge(misc_done, it * MISC + MISC0 + M_SCATTER + d + 1)
                    add(xT[:, d, :], xT[:, d, :], bank[b][:, 0:T]).then_inc(evicted[b], 1)
                low_experts(it, E_CHUNKS - 1 + AHEAD)
            dve.wait_ge(std_done, 7 * DEPTH + 1)
            link(dve.reciprocal(rstd[:, 0, :], bank[1][:, 0:T]))
            for d in range(KD):
                last = dve.scalar_tensor_tensor(out=uT[:, d, :], in0=xT[:, d, :], scalar=vecs[:, V_FIN + d:V_FIN + d + 1],
                                                in1=rstd[:, 0, :], op0=ALU.mult, op1=ALU.mult)
                last.then_inc(x_final, 1)

        @block.gpsimd
        def _(pool):
            order = [0]

            def link(ins):
                order[0] += 1
                ins.then_inc(pool_order, 1)
                pool.wait_ge(pool_order, order[0])

            def mul(out, x, y):
                return pool.tensor_tensor(out, x, y, ALU.mult)

            def product(out, x, y, t):
                link(mul(out[0], x[0], y[0]))
                link(mul(t, x[1], y[1]))
                link(pool.tensor_tensor(out[0], out[0], t, ALU.subtract))
                link(mul(out[1], x[0], y[1]))
                link(mul(t, x[1], y[0]))
                link(pool.tensor_tensor(out[1], out[1], t, ALU.add))

            link(pool.memset(s5m[0:GP, 0:G * P], 0.0))
            pool.dma_start(kscr.rearrange("g p x -> p g x")[:, :, 0:P],
                           s5m[0:GP, 0:G * P].rearrange("p (g x) -> p g x", g=G)).then_inc(zero_out, 16)
            pool.memset(xin[:, :, :], 0.0).then_inc(xin_zero, 1)
            pool.wait_ge(zero_out, 16)
            pool.wait_ge(consts_in, 16 * 7)
            pool.wait_ge(lam_ready, 2)
            for l in range(DEPTH):
                if l > 0:
                    pool.wait_ge(mm_done, DONE[(l - 1, "pr", KD - 1)])
                    pool.wait_ge(hstate_out, 32 * l)
                    for b in range(2):
                        pool.wait_ge(s_out[b], 64 * l)
                    pool.wait_ge(st_out, 16 * l)
                pool.dma_start(work[:, 0:1024], a["bc"][l]).then_inc(bc_in, 16)
                pool.dma_start(hst[:, :, :, NC:NC + NS], a["h0"][l]).then_inc(h0_in, 16)
                ls = slice(l * GJ, (l + 1) * GJ)
                link(pool.memset(pa[:, 0, 0, :], 1.0))
                link(pool.memset(pa[:, 1, 0, :], 0.0))
                link(pool.tensor_copy(pa[:, 0, 1, :], lw[:, 8, ls]))
                link(pool.tensor_copy(pa[:, 1, 1, :], lw[:, 9, ls]))

                def powers(lo, n, by):
                    x = [pa[:, r, lo:lo + n, :] for r in range(2)]
                    y = [pa[:, r, by:by + 1, :].broadcast_to([P, n, GJ]) for r in range(2)]
                    out = [pa[:, r, lo + by:lo + by + n, :] for r in range(2)]
                    product(out, x, y, pw[:, 0, 0:n, :])

                powers(1, 1, 1)
                powers(1, 2, 2)
                powers(1, 4, 4)
                for s in range(S):
                    link(pool.tensor_copy(pd[:, :, s, :], pa[:, :, S - 1 - s, :]))
                for w, r in ((0, 0), (1, 0), (3, 1)):
                    link(pool.tensor_copy(l8[:, w, :], pa[:, r, S, :]))
                pool.tensor_scalar(l8[:, 2, :], pa[:, 1, S, :], -1.0, 0.0, ALU.mult, ALU.add).then_inc(l8_ready, 1)
                pool.wait_ge(bc_in, 16 * (l + 1))
                flat = [P, GJ, GP]
                f = [lw[:, w, ls].unsqueeze(2).broadcast_to(flat) for w in (12, 13)]
                t = pt1[:, 0:GJ * GP].rearrange("p (j q) -> p j q", j=GJ)
                product([bb[:, r] for r in range(2)], f, [bc[:, r] for r in range(2)], t)
                wide = [P, GJ, S, GP]
                x = [pd[:, r].rearrange("p s j -> p j s").unsqueeze(3).broadcast_to(wide) for r in range(2)]
                y = [bb[:, r].unsqueeze(2).broadcast_to(wide) for r in range(2)]
                t = pt1[:, 0:GJ * S * GP].rearrange("p (j s q) -> p j s q", j=GJ, s=S)
                product([gb[:, :, r] for r in range(2)], x, y, t)
                wide = [P, GJ, S + 1, GP]
                x = [pa[:, r].rearrange("p k j -> p j k").unsqueeze(3).broadcast_to(wide) for r in range(2)]
                y = [bc[:, 2 + r].unsqueeze(2).broadcast_to(wide) for r in range(2)]
                t = pt1[:, 0:GJ * 9 * GP].rearrange("p (j s q) -> p j s q", j=GJ, s=9)
                product([v.rearrange("p j (k q) -> p j k q", q=GP) for v in (clr, cli)], x, y, t)
                link(pool.tensor_scalar(cli[:, :, :], cli[:, :, :], -1.0, 0.0, ALU.mult, ALU.add))
                few = [GP, G, GP]
                mul(dd, ident[0:GP, 0:GP].unsqueeze(1).broadcast_to(few), dskip[:, l, :].unsqueeze(2).broadcast_to(few)
                    ).then_inc(gb_ready, 1)
                if l > 0:
                    pool.wait_ge(mm_done, DONE[(l - 1, "dn", 7)])
                pool.dma_start(xs[:, :, :, 0:TAPS - 1], a["convst"][l]).then_inc(conv_state_in, 16)
                for i in range(8):
                    pool.wait_ge(*out_of((l, "kk", i)))
                pool.wait_ge(gb_ready, l + 1)
                pool.tensor_tensor(toep[0:GP, :, 0:GP], toep[0:GP, :, 0:GP], dd, ALU.add).then_inc(kmat_ready, 1)
                pool.wait_ge(kmat_ready, l + 1)
                pool.dma_start(kscr.rearrange("g p x -> p g x")[:, :, P:2 * P], toep[0:GP, :, :]).then_inc(kscr_out, 16)
                for b in range(2):
                    pool.dma_start(sring[:, b, :, :], a["sret"][l, b].rearrange("h d v -> d h v")).then_inc(s_in[b], 16)
                pool.wait_ge(kscr_out, 16 * (l + 1))
                for s in range(S):
                    pool.dma_start(toep[s * GP:(s + 1) * GP, :, :],
                                   kscr.rearrange("g p x -> p g x")[:, :, P - GP * s:2 * P - GP * s]).then_inc(toep_in, 16)
                for m in range(4):
                    pool.wait_ge(*out_of((l, "ca", m)))
                pool.wait_ge(conv_state_in, 16 * (l + 1))
                pool.dma_start(a["conv_p"][l], xc[:, :, SEQ:SEQ + TAPS - 1]).then_inc(conv_state_out, 16)
                pool.dma_start(a["conv_s"][l], xs[:, :, :, 1:TAPS]).then_inc(conv_state_out, 16)
                for h in range(HEADS):
                    pool.wait_ge(*out_of((l, "st", h)))
                pool.dma_start(a["ret_p"][l].rearrange("h d v -> d h v"), stst[:, :, :]).then_inc(st_out, 16)
                for b in range(NS):
                    pool.wait_ge(*out_of((l, "oa", b)))
                    pool.wait_ge(*out_of((l, "ob", b)))
                    pool.dma_start(a["ret_s"][l, b].rearrange("h d v -> d h v"), sring[:, b % 2, :, :]).then_inc(s_out[b % 2], 16)
                    if b + 2 < NS:
                        pool.wait_ge(mm_done, DONE[(l, "os", b)])
                        pool.wait_ge(s_out[b % 2], 16 * (4 * l + b // 2 + 1))
                        pool.dma_start(sring[:, b % 2, :, :], a["sret"][l, b + 2].rearrange("h d v -> d h v")).then_inc(s_in[b % 2], 16)
                pool.wait_ge(h_ready, l + 1)
                pool.dma_start(a["h_p"][l], hfin[:, :, :]).then_inc(hstate_out, 16)
                pool.dma_start(a["h_s"][l], hnew[:, :, :, :]).then_inc(hstate_out, 16)
            pool.wait_ge(hstate_out, 32 * DEPTH)
            pool.wait_ge(conv_state_out, 32 * DEPTH)
            pool.wait_ge(st_out, 16 * DEPTH)
            for b in range(2):
                pool.wait_ge(s_out[b], 64 * DEPTH)


def _blocks(w):
    k, m = w.shape
    return w.reshape(k // P, P, m // P, P).transpose(2, 0, 1, 3)


def _stream(parts):
    b = np.concatenate([p.reshape(-1, P, P) for p in parts])
    return b.reshape(-1, CH, P, P).transpose(0, 2, 1, 3).reshape(-1, P, CH * P)


def _pairs(x, y):
    return [z for pair in zip(x, y) for z in pair]


def _wide(w):
    return w.reshape(2, 4, P, -1, WIDE).transpose(3, 0, 2, 1, 4).reshape(-1, 2, P, 4 * WIDE)


def _channels(x):
    return x.reshape(x.shape[0], -1, P).transpose(2, 1, 0)


def _column(v):
    return v.reshape(-1, P).T


def kernel(**inputs):
    import concourse.bacc as bacc
    from concourse import mybir
    from concourse.bass_utils import run_bass_kernel_spmd as run

    x = {k: np.asarray(v) for k, v in inputs.items()}
    F32 = np.float32

    chunks = []
    for l in range(DEPTH):
        w = _blocks(x["w_in"][l])
        parts = [w[32:36], w[28:32], w[0:4], w[4:8], w[8:12], w[12:20]]
        parts += _pairs(w[52:60], _blocks(x["conv_proj"][l]))
        parts += [w[20:28]]
        parts += _pairs(w[44:52], _blocks(x["ret_proj"][l]))
        parts += [_blocks(x["s5_glu_w"][l])]
        parts += _pairs(w[36:44], _blocks(x["s5_proj"][l]))
        parts += [_blocks(x["w_out"][l])]
        if l == 0:
            parts += _pairs(_blocks(x["ffn_w_gate"][0]), _blocks(x["ffn_w_up"][0]))
            parts += [_blocks(x["ffn_w_down"][0])]
        chunks.append(_stream(parts))
    experts = []
    for e in range(NEXP):
        experts.append(np.stack([_wide(x["moe_w_gate"][0, e]), _wide(x["moe_w_up"][0, e])], axis=1).reshape(GU, P, 2048))
        experts.append(x["moe_w_down"][0, e].reshape(DN, 2, P, D).transpose(0, 2, 1, 3).reshape(DN, P, 2048))

    def groups(v):
        v = v.reshape((2, GJ) + v.shape[1:])
        return np.moveaxis(v, 1, 2).reshape((P, GJ) + v.shape[3:])

    f = {}
    f["weights"] = np.concatenate(chunks)
    f["experts"] = np.concatenate(experts)
    f["xT"] = np.concatenate([_channels(x["x_prompt"][0]), _channels(x["x_sample"][:, 0])], axis=2)
    f["vecs"] = np.concatenate([c for l in range(DEPTH) for c in (
        _column(x["norm_mix_g"][l]), _column(x["norm_ffn_g"][l]), _column(x["conv_pw_b"][l]),
        _channels(x["conv_dw_w"][l]).reshape(P, -1), _column(x["conv_dw_b"][l]), _column(x["conv_ln_g"][l]),
        _column(x["conv_ln_b"][l]), _column(x["s5_glu_b"][l]))] + [_column(x["norm_final_g"])], axis=1)
    rows = [x["s5_lambda_re"], x["s5_lambda_im"], np.repeat(x["s5_log_dt"][:, :, None], 64, axis=2)]
    f["lam"] = np.stack([np.concatenate([groups(r[l]) for l in range(DEPTH)], axis=1) for r in rows], axis=1)
    f["dskip"] = np.stack([x["s5_d"][l].reshape(G, GP).T for l in range(DEPTH)], axis=1)
    f["bc"] = np.stack([np.concatenate([
        groups(x["s5_b_re"][l]).reshape(P, -1), groups(x["s5_b_im"][l]).reshape(P, -1),
        groups(x["s5_c_re"][l].transpose(0, 2, 1)).reshape(P, -1), groups(x["s5_c_im"][l].transpose(0, 2, 1)).reshape(P, -1),
    ], axis=1) for l in range(DEPTH)])
    f["h0"] = np.stack([np.stack([groups(x[n][l].transpose(1, 2, 0)) for n in ("state_s5_re", "state_s5_im")], axis=1)
                        for l in range(DEPTH)])
    f["convst"] = np.stack([x["state_conv"][l].reshape(NS, TAPS - 1, 4, P).transpose(3, 2, 0, 1) for l in range(DEPTH)])
    f["sret"] = x["state_ret"]
    f["router"] = x["moe_router"][0].reshape(KD, P, NEXP).transpose(1, 0, 2)

    half = P // 2
    freqs = F32(10000.0) ** (-np.arange(half, dtype=F32) / F32(half))
    pos = np.concatenate([np.arange(SEQ), np.full(NS, 2048)]).astype(F32)
    ang = (pos[None, :] * freqs[:, None]).astype(F32).astype(np.float64)
    cos = np.concatenate([np.cos(ang), np.cos(ang)])
    sin = np.concatenate([np.sin(ang), -np.sin(ang)])
    f["rope"] = np.stack([cos, sin], axis=1).astype(F32)
    gamma = 1.0 - 2.0 ** (-5.0 - np.arange(HEADS))
    j, i = np.arange(P)[:, None], np.arange(SEQ)[None, :]
    f["decay"] = np.stack([np.where(i >= j, g ** np.maximum(i - j, 0), 0.0) for g in gamma], axis=1).astype(F32)
    f["kdec"] = np.stack([np.stack([g ** (SEQ - 1 - it * P - np.arange(P)) for g in gamma], axis=1) for it in range(2)], axis=1).astype(F32)
    f["ident"] = np.eye(P, dtype=F32)
    f["tri"] = np.triu(np.ones((P, P), F32), 1)
    f["iota"] = np.tile(np.arange(CAP, dtype=F32), (P, 1))

    outs = {"y": (P, KD, T), "h_p": (DEPTH, P, 2, GJ), "h_s": (DEPTH, P, 2, GJ, NS),
            "ret_p": (DEPTH, HEADS, P, DV), "ret_s": (DEPTH, NS, HEADS, P, DV),
            "conv_p": (DEPTH, P, 4, TAPS - 1), "conv_s": (DEPTH, P, 4, NS, TAPS - 1)}

    nc = bacc.Bacc("TRN2", target_bir_lowering=False, num_devices=1)
    arrays, args = {}, {}
    for name, v in f.items():
        v = np.ascontiguousarray(v)
        arrays["in_" + name] = v
        args[name] = nc.dram_tensor("in_" + name, v.shape, mybir.dt.from_np(v.dtype), kind="ExternalInput").ap()
    for name, shape in outs.items():
        args[name] = nc.dram_tensor("out_" + name, shape, mybir.dt.float32, kind="ExternalOutput").ap()
    build(nc, args)
    r = run(nc, [arrays], core_ids=[0]).results[0]
    o = {name: r["out_" + name] for name in outs}

    y = o["y"].transpose(2, 1, 0).reshape(T, D)

    def ungroup(v):
        return v.reshape(DEPTH, 2, 64, GJ).transpose(0, 1, 3, 2).reshape(DEPTH, G, 64)

    h_p = [ungroup(o["h_p"][:, :, r]).reshape(DEPTH, 1, G, 64) for r in range(2)]
    h_s = [np.stack([ungroup(o["h_s"][:, :, r, :, b]) for b in range(NS)], axis=1) for r in range(2)]
    conv_p = o["conv_p"].transpose(0, 3, 2, 1).reshape(DEPTH, 1, TAPS - 1, 4 * P)
    conv_s = o["conv_s"].transpose(0, 3, 4, 2, 1).reshape(DEPTH, NS, TAPS - 1, 4 * P)
    return (y[None, :SEQ], y[SEQ:, None, :], h_p[0], h_p[1], o["ret_p"].reshape(DEPTH, 1, HEADS, P, DV), conv_p,
            h_s[0], h_s[1], o["ret_s"], conv_s)
```
